# Optimizing a Trainium2 kernel written in Bass

```python
import math
import jax
import jax.numpy as jnp
from jax import lax
import numpy as np

D_MODEL = 1024
BATCH = 1
SEQ = 512
DEPTH = 2
DEC_BATCH = 8
DEC_SEQ = 8
PAST_LEN = 2048
PAGE_SIZE = 128

N_HEADS = 16
HEAD_DIM = D_MODEL // N_HEADS
KV_HEADS = 2
GROUP = N_HEADS // KV_HEADS
IDX_HEADS = 8
IDX_DIM = 64
TOPK_MAX = 256
WINDOW = 128
N_BUCKETS = 32
MAX_DISTANCE = 128
D_FF = 2688
RMS_EPS = 1e-6
Q_BLOCK = 128
N_A_LAYERS = (DEPTH + 1) // 2
N_B_LAYERS = DEPTH // 2
QW = N_HEADS * HEAD_DIM
KVW = KV_HEADS * HEAD_DIM
A_SPLITS = (QW, QW + KVW, QW + 2 * KVW, QW + 2 * KVW + IDX_HEADS * IDX_DIM,
            QW + 2 * KVW + IDX_HEADS * IDX_DIM + IDX_DIM)
A_IN = A_SPLITS[-1] + IDX_HEADS
B_SPLITS = (QW, QW + KVW)
B_IN = QW + 2 * KVW
NEG = float(np.finfo(np.float32).min)

kernel_name = 'hybrid_dsa_swa_macaron_step'

def rmsnorm(x, g):
    xf = x.astype(jnp.float32)
    y = xf * lax.rsqrt(jnp.mean(xf * xf, axis=-1, keepdims=True) + RMS_EPS)
    return (y * g.astype(jnp.float32)).astype(x.dtype)

def swiglu(h, w_gate, w_up, w_down):
    return (jax.nn.silu(h @ w_gate) * (h @ w_up)) @ w_down

def t5_bucket(dist):
    n = jnp.maximum(dist, 0)
    max_exact = N_BUCKETS // 2
    nf = jnp.maximum(n, 1).astype(jnp.float32)
    log_part = jnp.log(nf / max_exact) / math.log(MAX_DISTANCE / max_exact) * (N_BUCKETS - max_exact)
    large = jnp.minimum(max_exact + log_part.astype(jnp.int32), N_BUCKETS - 1)
    return jnp.where(n < max_exact, n, large)

def rel_bias(dist, table):
    return table[t5_bucket(dist)].astype(jnp.float32)

def sink_softmax(logits, sinks):
    s = sinks.astype(jnp.float32).reshape(KV_HEADS, GROUP, 1, 1)
    m = jnp.maximum(jnp.max(logits, axis=-1, keepdims=True), s)
    e = jnp.exp(logits - m)
    return e / (jnp.sum(e, axis=-1, keepdims=True) + jnp.exp(s - m))

def split_a(h, w_in):
    lead = h.shape[:-1]
    q, k, v, qi, ki, wi = jnp.split(h @ w_in, A_SPLITS, axis=-1)
    return (q.reshape(*lead, KV_HEADS, GROUP, HEAD_DIM), k.reshape(*lead, KV_HEADS, HEAD_DIM),
            v.reshape(*lead, KV_HEADS, HEAD_DIM), qi.reshape(*lead, IDX_HEADS, IDX_DIM), ki, wi)

def split_b(h, w_in):
    lead = h.shape[:-1]
    q, k, v = jnp.split(h @ w_in, B_SPLITS, axis=-1)
    return (q.reshape(*lead, KV_HEADS, GROUP, HEAD_DIM), k.reshape(*lead, KV_HEADS, HEAD_DIM),
            v.reshape(*lead, KV_HEADS, HEAD_DIM))

def indexer_scores(qi, wi, ki):
    dots = jnp.einsum('bthd,bsd->bths', qi, ki).astype(jnp.float32) * IDX_DIM ** -0.5
    return jnp.einsum('bths,bth->bts', jax.nn.relu(dots), wi.astype(jnp.float32) * IDX_HEADS ** -0.5)

def sparse_attend(q, k_sel, v_sel, dist, table):
    bias = rel_bias(dist, table)
    bias = jnp.moveaxis(bias.reshape(*bias.shape[:-1], KV_HEADS, GROUP), -3, -1)
    logits = jnp.einsum('btngd,btjnd->btngj', q, k_sel).astype(jnp.float32) * HEAD_DIM ** -0.5 + bias
    logits = jnp.where((dist >= 0)[:, :, None, None, :], logits, NEG)
    p = jax.nn.softmax(logits, axis=-1).astype(v_sel.dtype)
    o = jnp.einsum('btngj,btjnd->btngd', p, v_sel)
    return o.reshape(*o.shape[:2], QW)

def dsa_prompt(h, w_in, w_out, table):
    b, t, _ = h.shape
    q, k, v, qi, ki, wi = split_a(h, w_in)
    topk = min(TOPK_MAX, t // 4)
    n_blk = t // Q_BLOCK
    key_pos = jnp.arange(t, dtype=jnp.int32)
    bidx = jnp.arange(b)[:, None, None]

    def to_blocks(a):
        return jnp.moveaxis(a.reshape(b, n_blk, Q_BLOCK, *a.shape[2:]), 1, 0)

    def block(args):
        qb, qib, wib, qpos = args
        scores = indexer_scores(qib, wib, ki)
        scores = jnp.where(key_pos[None, None, :] <= qpos[None, :, None], scores, NEG)
        _, sel = lax.top_k(scores, topk)
        dist = qpos[None, :, None] - sel
        return sparse_attend(qb, k[bidx, sel], v[bidx, sel], dist, table)

    out = lax.map(block, (to_blocks(q), to_blocks(qi), to_blocks(wi), key_pos.reshape(n_blk, Q_BLOCK)))
    out = jnp.moveaxis(out, 0, 1).reshape(b, t, QW)
    return out @ w_out, jnp.stack([k, v], axis=2), ki

def dsa_sample(h, cache_kv, cache_idx, layer, page_table, w_in, w_out, table):
    b, tn, _ = h.shape
    past = page_table.shape[1] * PAGE_SIZE
    topk = min(TOPK_MAX, (past + tn) // 4)
    q, k, v, qi, ki, wi = split_a(h, w_in)
    kv_new = jnp.stack([k, v], axis=2)
    ki_all = jnp.concatenate([cache_idx[layer, page_table].reshape(b, past, IDX_DIM), ki], axis=1)
    qpos = past + jnp.arange(tn, dtype=jnp.int32)
    key_pos = jnp.arange(past + tn, dtype=jnp.int32)
    scores = indexer_scores(qi, wi, ki_all)
    scores = jnp.where(key_pos[None, None, :] <= qpos[None, :, None], scores, NEG)
    _, sel = lax.top_k(scores, topk)
    bidx = jnp.arange(b)[:, None, None]
    sel_past = jnp.minimum(sel, past - 1)
    phys = page_table[bidx, sel_past // PAGE_SIZE]
    kv_past = cache_kv[layer, phys, sel_past % PAGE_SIZE]
    kv_cur = kv_new[bidx, jnp.clip(sel - past, 0, tn - 1)]
    kv_sel = jnp.where((sel < past)[..., None, None, None], kv_past, kv_cur)
    dist = qpos[None, :, None] - sel
    out = sparse_attend(q, kv_sel[..., 0, :, :], kv_sel[..., 1, :, :], dist, table)
    return out @ w_out, kv_new, ki

def swa_prompt(h, w_in, w_out, sinks, table):
    b, t, _ = h.shape
    n_blk = t // WINDOW
    q, k, v = split_b(h, w_in)
    qb = q.reshape(b, n_blk, WINDOW, KV_HEADS, GROUP, HEAD_DIM)

    def band(a):
        ab = a.reshape(b, n_blk, WINDOW, KV_HEADS, HEAD_DIM)
        prev = jnp.concatenate([jnp.zeros_like(ab[:, :1]), ab[:, :-1]], axis=1)
        return jnp.concatenate([prev, ab], axis=2)

    kb, vb = band(k), band(v)
    qloc = jnp.arange(WINDOW, dtype=jnp.int32)[:, None] + WINDOW
    kloc = jnp.arange(2 * WINDOW, dtype=jnp.int32)[None, :]
    dist = qloc - kloc
    valid = (dist >= 0) & (dist <= WINDOW)
    first = (jnp.arange(n_blk) == 0)[:, None, None]
    valid = valid[None] & ~(first & (kloc < WINDOW)[None])
    bias = jnp.transpose(rel_bias(dist, table).reshape(WINDOW, 2 * WINDOW, KV_HEADS, GROUP), (2, 3, 0, 1))
    logits = jnp.einsum('bcqngd,bcknd->bcngqk', qb, kb).astype(jnp.float32) * HEAD_DIM ** -0.5 + bias
    logits = jnp.where(valid[None, :, None, None], logits, NEG)
    p = sink_softmax(logits, sinks).astype(vb.dtype)
    o = jnp.einsum('bcngqk,bcknd->bcqngd', p, vb).reshape(b, t, QW)
    kv = jnp.stack([k, v], axis=2)
    return o @ w_out, kv[:, t - WINDOW:]

def swa_sample(h, state, past, w_in, w_out, sinks, table):
    b, tn, _ = h.shape
    q, k, v = split_b(h, w_in)
    kv_all = jnp.concatenate([state, jnp.stack([k, v], axis=2)], axis=1)
    qpos = past + jnp.arange(tn, dtype=jnp.int32)
    kpos = past - WINDOW + jnp.arange(WINDOW + tn, dtype=jnp.int32)
    dist = qpos[:, None] - kpos[None, :]
    valid = (dist >= 0) & (dist <= WINDOW)
    bias = jnp.transpose(rel_bias(dist, table).reshape(tn, WINDOW + tn, KV_HEADS, GROUP), (2, 3, 0, 1))
    logits = jnp.einsum('bqngd,bknd->bngqk', q, kv_all[:, :, 0]).astype(jnp.float32) * HEAD_DIM ** -0.5 + bias
    logits = jnp.where(valid, logits, NEG)
    p = sink_softmax(logits, sinks).astype(kv_all.dtype)
    o = jnp.einsum('bngqk,bknd->bqngd', p, kv_all[:, :, 1]).reshape(b, tn, QW)
    return o @ w_out, kv_all[:, tn:]

def setup_inputs(seed: int = 0) -> dict:
    key = jax.random.key(seed)
    ks = jax.random.split(key, 18)
    n_pages = PAST_LEN // PAGE_SIZE
    n_pool = (5 * DEC_BATCH * n_pages) // 4

    def nrm(k, shape, scale=1.0):
        return jax.random.normal(k, shape, jnp.float32) * scale

    page_table = jax.random.permutation(ks[5], n_pool)[:DEC_BATCH * n_pages].reshape(DEC_BATCH, n_pages).astype(jnp.int32)
    return {
        'x_prompt': nrm(ks[0], (BATCH, SEQ, D_MODEL)),
        'x_sample': nrm(ks[1], (DEC_BATCH, DEC_SEQ, D_MODEL)),
        'cache_kv': nrm(ks[2], (N_A_LAYERS, n_pool, PAGE_SIZE, 2, KV_HEADS, HEAD_DIM)),
        'cache_idx': nrm(ks[3], (N_A_LAYERS, n_pool, PAGE_SIZE, IDX_DIM)),
        'state_win_kv': nrm(ks[4], (N_B_LAYERS, DEC_BATCH, WINDOW, 2, KV_HEADS, HEAD_DIM)),
        'page_table': page_table,
        'rel_bias': nrm(ks[6], (N_BUCKETS, N_HEADS), 0.5),
        'ffn_norm': 1.0 + nrm(ks[7], (DEPTH, 2, D_MODEL), 0.1),
        'ffn_w_gate': nrm(ks[8], (DEPTH, 2, D_MODEL, D_FF), D_MODEL ** -0.5),
        'ffn_w_up': nrm(ks[9], (DEPTH, 2, D_MODEL, D_FF), D_MODEL ** -0.5),
        'ffn_w_down': nrm(ks[10], (DEPTH, 2, D_FF, D_MODEL), D_FF ** -0.5),
        'mix_norm': 1.0 + nrm(ks[11], (DEPTH, D_MODEL), 0.1),
        'a_w_in': nrm(ks[12], (N_A_LAYERS, D_MODEL, A_IN), D_MODEL ** -0.5),
        'a_w_out': nrm(ks[13], (N_A_LAYERS, QW, D_MODEL), QW ** -0.5),
        'b_w_in': nrm(ks[14], (N_B_LAYERS, D_MODEL, B_IN), D_MODEL ** -0.5),
        'b_w_out': nrm(ks[15], (N_B_LAYERS, QW, D_MODEL), QW ** -0.5),
        'b_sinks': nrm(ks[16], (N_B_LAYERS, N_HEADS)),
        'final_norm': 1.0 + nrm(ks[17], (D_MODEL,), 0.1),
    }

def reference(x_prompt, x_sample, cache_kv, cache_idx, state_win_kv, page_table, rel_bias, ffn_norm,
              ffn_w_gate, ffn_w_up, ffn_w_down, mix_norm, a_w_in, a_w_out, b_w_in, b_w_out, b_sinks, final_norm):
    past = page_table.shape[1] * PAGE_SIZE
    xp, xs = x_prompt, x_sample
    kv_p, idx_p, win_p, kv_s, idx_s, win_s = [], [], [], [], [], []
    for i in range(DEPTH):
        xp = xp + 0.5 * swiglu(rmsnorm(xp, ffn_norm[i, 0]), ffn_w_gate[i, 0], ffn_w_up[i, 0], ffn_w_down[i, 0])
        xs = xs + 0.5 * swiglu(rmsnorm(xs, ffn_norm[i, 0]), ffn_w_gate[i, 0], ffn_w_up[i, 0], ffn_w_down[i, 0])
        hp = rmsnorm(xp, mix_norm[i])
        hs = rmsnorm(xs, mix_norm[i])
        j = i // 2
        if i % 2 == 0:
            yp, kvp, kip = dsa_prompt(hp, a_w_in[j], a_w_out[j], rel_bias)
            ys, kvs, kis = dsa_sample(hs, cache_kv, cache_idx, j, page_table, a_w_in[j], a_w_out[j], rel_bias)
            kv_p.append(kvp)
            idx_p.append(kip)
            kv_s.append(kvs)
            idx_s.append(kis)
        else:
            yp, wp = swa_prompt(hp, b_w_in[j], b_w_out[j], b_sinks[j], rel_bias)
            ys, ws = swa_sample(hs, state_win_kv[j], past, b_w_in[j], b_w_out[j], b_sinks[j], rel_bias)
            win_p.append(wp)
            win_s.append(ws)
        xp = xp + yp
        xs = xs + ys
        xp = xp + 0.5 * swiglu(rmsnorm(xp, ffn_norm[i, 1]), ffn_w_gate[i, 1], ffn_w_up[i, 1], ffn_w_down[i, 1])
        xs = xs + 0.5 * swiglu(rmsnorm(xs, ffn_norm[i, 1]), ffn_w_gate[i, 1], ffn_w_up[i, 1], ffn_w_down[i, 1])
    y_prompt = rmsnorm(xp, final_norm)
    y_sample = rmsnorm(xs, final_norm)
    return (y_prompt, y_sample, jnp.stack(kv_p), jnp.stack(idx_p), jnp.stack(win_p),
            jnp.stack(kv_s), jnp.stack(idx_s), jnp.stack(win_s))


_drawn_inputs = setup_inputs


def setup_inputs(seed=0):
    import zlib

    import numpy as np

    out = dict(_drawn_inputs(seed))
    spreads = {}
    factors = {'b_sinks': 5.248}
    for name, (base, spread) in spreads.items():
        noise = np.random.default_rng([zlib.crc32(name.encode()), seed]).standard_normal(out[name].shape)
        drawn = base * np.exp(spread * noise) if base else spread * noise
        out[name] = jnp.asarray(drawn.astype(out[name].dtype))
    for name, factor in factors.items():
        out[name] = (out[name] * factor).astype(out[name].dtype)
    return out
```

```python
import math
from contextlib import ExitStack

import concourse.bass as bass
import numpy as np
from concourse import mybir

F32 = mybir.dt.float32
F32R = mybir.dt.float32r
BF16 = mybir.dt.bfloat16
ALU = mybir.AluOpType
ACT = mybir.ActivationFunctionType
AX = mybir.AxisListType.X

P = 128
D = 1024
ND = D // P
SEQ = 512
NQT = SEQ // P
NB, NT = 8, 8
NS = NB * NT
TOK = SEQ + NS
HALF = TOK // 2
NTT = -(-TOK // P)
FF = 2688
NF = FF // P
HEADS, HD, KVH = 16, 64, 2
GRP = HEADS // KVH
IH, IDIM = 8, 64
PAST, PAGE = 2048, 128
NPG = PAST // PAGE
NPOOL = 5 * NB * NPG // 4
KEYS = PAST + NT
NEAR = P + NT
TOPK_P = min(256, SEQ // 4)
TOPK_S = min(256, KEYS // 4)
QW, KVW = HEADS * HD, KVH * HD
A_IN = QW + 2 * KVW + IH * IDIM + IDIM + IH
EPS = 1e-6
MASK = -1.0e30
TAKEN = -3.0e38
NBUCK, MAXD = 32, 128
GW = 3 * P

SKEW = HEADS * GW

RING = 3
DB = NF // RING
GU_CHUNKS, DN_CHUNKS = 2 * NF, ND * RING
A_CHUNKS, B_CHUNKS = 1 + IH // 2 + 2 + GRP, 2 + GRP


def layout():
    at, chunk, acc, event = {}, 0, 0, 1
    for name, chunks, accs, events in (
            ("ffn0", GU_CHUNKS + DN_CHUNKS, GU_CHUNKS, 1), ("inA", A_CHUNKS, A_CHUNKS, 0), ("outA", ND, 0, 1),
            ("ffn1", GU_CHUNKS + DN_CHUNKS, GU_CHUNKS, 1), ("ffn2", GU_CHUNKS + DN_CHUNKS, GU_CHUNKS, 1),
            ("inB", B_CHUNKS, B_CHUNKS, 0), ("outB", ND, 0, 1), ("ffn3", GU_CHUNKS + DN_CHUNKS, GU_CHUNKS, 1)):
        at[name] = (chunk, acc, event)
        chunk, acc, event = chunk + chunks, acc + accs, event + events
    return at


class Steps:

    def __init__(self, eng, sem):
        self.eng, self.sem, self.n, self.i, self.per = eng, sem, 0, None, 0

    def mark(self, ins):
        ins.then_inc(self.sem, 1)
        self.n += 1

    def settle(self):
        self.eng.wait_ge(self.sem, self.n if self.i is None else self.i * self.per + self.n)

    def done(self, ins):
        self.mark(ins)
        self.settle()


    def loop(self, i, per):
        self.i, self.per, self.first = i, per, self.n

    def end(self, times):
        assert self.n == self.first + self.per
        self.n, self.i = self.first + self.per * times, None


def mixer_memory(sb, L):
    m = {}

    def mb(c, name, shape, dt=F32):
        m[name] = sb(c, name + L, shape, dt)

    with ExitStack() as c:
        mb(c, "kT", [P, TOK])
        mb(c, "kvtok", [P, NTT, 2 * KVW])
        mb(c, "vnew", [NT, NB, KVW])
        mb(c, "biasS", [P, NEAR])
        mb(c, "nm", [P, NQT, KVH, GRP])
        mb(c, "rs", [P, NQT, KVH, GRP])
        mb(c, "ri", [P, NQT, KVH, GRP])
        mb(c, "es", [P, KVH, GRP])
        mb(c, "nsink", [P, KVH, GRP])
        mb(c, "nmS", [P, NB])
        mb(c, "rsS", [P, NB])
        mb(c, "riS", [P, NB])
        mb(c, "esS", [P, NB])
        mb(c, "nsinkS", [P, 1])
        mb(c, "mx8", [P, 8])
        if L == "A":
            mb(c, "pmask", [P, NQT - 1, SEQ], BF16)
            mb(c, "scs", [NS, KEYS])
            with ExitStack() as c2:
                mb(c2, "kic", [P, NB, NPG // 2, PAGE])
            with ExitStack() as c2:
                mb(c2, "kv0", [P, NPG, 2 * KVW])
                mb(c2, "kv1", [P, NPG, 2 * KVW])
            with ExitStack() as c2:
                mb(c2, "scp", [P, NQT - 1, SEQ])
                mb(c2, "scp_pad", [P, NPG * 2 * KVW - (NQT - 1) * SEQ])
                mb(c2, "p", [P, 2, KVH, SEQ])
                mb(c2, "pt", [P, KVH, NQT, P])
                mb(c2, "otok", [P, GRP, KVH, HD])
            mb(c, "kvroom", [P, 2 * NPG * 2 * KVW])
            mb(c, "maskS", [NS, KEYS], BF16)
            mb(c, "selb", [NS, NB, P], BF16)
            mb(c, "qbd", [P, NB, P])
            with ExitStack() as c2:
                mb(c2, "kist", [P, 2, NPG, IDIM])
            with ExitStack() as c2:
                mb(c2, "qT", [P, GRP, TOK])
                with ExitStack() as c3:
                    mb(c3, "strip", [P, KVH, GRP, 2 * P])
                with ExitStack() as c3:
                    mb(c3, "vT", [P, TOK])
                    mb(c3, "kiT", [P, TOK])
                    mb(c3, "qiT", [P, IH // 2, TOK])
                    mb(c3, "qiS", [P, NB, IH, NT])
                    mb(c3, "r", [P, 2, SEQ])
                    mb(c3, "kiw", [P, NTT, IDIM + IH])
                    mb(c3, "wis", [P, NQT, IH])
                    mb(c3, "wbl", [P, NB // 2, NS])
                    mb(c3, "pairm", [P, NB // 2, NS])
                    mb(c3, "cmask", [P, P])
                    mb(c3, "rep", [P, P])
                    mb(c3, "tailm", [NS, NT])
            with ExitStack() as c2:
                mb(c2, "KT", [P, 2, PAST])
                mb(c2, "ps", [P, KEYS])
                mb(c2, "pts", [P, NPG + 1, P])
                mb(c2, "os", [P, P])
        else:
            mb(c, "kv", [P, NB, 2 * KVW])
            mb(c, "qbd", [P, NB, P])
            mb(c, "wm", [P, P])
            mb(c, "wmS", [P, NEAR])
            mb(c, "qT", [P, GRP, TOK])
            mb(c, "strip", [P, KVH, GRP, 2 * P])
            mb(c, "vT", [P, TOK])
            mb(c, "p", [P, 2, KVH, SEQ])
            mb(c, "pt", [P, KVH, NQT, P])
            mb(c, "otok", [P, GRP, KVH, HD])
            mb(c, "KT", [P, 2, P])
            mb(c, "ps", [P, NEAR])
            mb(c, "pts", [P, 2, P])
            mb(c, "os", [P, P])
    return m


def bass_hybrid_step(nc, io):
    at = layout()
    ctx = ExitStack()
    with ctx:
        def sb(c, name, shape, dt=F32):
            return c.enter_context(nc.sbuf_tensor(name, shape, dt))

        def sem(name):
            return ctx.enter_context(nc.semaphore(name))

        X = sb(ctx, "X", [P, ND, TOK])
        XH = sb(ctx, "XH", [P, ND, TOK], F32R)
        XL = sb(ctx, "XL", [P, ND, TOK], F32R)
        WST = [sb(ctx, f"WST{s}", [P, ND * P]) for s in range(RING)]
        WSP = [sb(ctx, f"WSP{s}", [P, 2, ND * P], F32R) for s in range(RING)]
        rstd = sb(ctx, "rstd", [P, TOK])
        ssum = sb(ctx, "ssum", [P, TOK])
        sq = sb(ctx, "sq", [P, TOK])
        ident = sb(ctx, "ident", [P, P])
        identb = sb(ctx, "identb", [P, P], BF16)
        ones = sb(ctx, "ones", [P, P])
        gains = sb(ctx, "gains", [P, 7 * ND])
        warm = sb(ctx, "warm", [P, 4])

        with ExitStack() as c:
            GH = sb(c, "GH", [P, NF, TOK], F32R)
            GL = sb(c, "GL", [P, NF, TOK], F32R)
            gs = sb(c, "gs", [P, 2, TOK])
            us = sb(c, "us", [P, TOK])
        with ExitStack() as c:
            xtok = sb(c, "xtok", [P, NTT, D])
            grows = sb(c, "grows", [7 * ND, P])
            tabx = sb(c, "tabx", [NBUCK + 1, HEADS])
            coef = sb(c, "coef", [NBUCK + 1, GW])
            gvec = sb(c, "gvec", [HEADS, GW])


        mixers = {L: mixer_memory(sb, L) for L in "AB"}
        psum = ctx.enter_context(nc.psum_tensor("psum", [P, 8, SEQ], F32))
        bank = [psum[:, k, :] for k in range(8)]
        PS = [psum[:, 2 * k:2 * k + 2, :] for k in range(4)]
        sample_logits = psum[:, 0:5, :].rearrange("p k c -> p (k c)")
        gscr = nc.dram_tensor("gscr", [P * (SKEW + 1)], F32, kind="Internal")

        stage_in = [sem(f"stage_in{s}") for s in range(RING)]
        w_hi, w_split, w_used = sem("w_hi"), sem("w_split"), sem("w_used")
        acc_evac = sem("acc_evac")
        silu_done, gh_ready = sem("silu_done"), sem("gh_ready")
        x_upd, sq_done, ssum_done = sem("x_upd"), sem("sq_done"), sem("ssum_done")
        xh_done, xl_done = sem("xh_done"), sem("xl_done")
        stat_done, var_done, sd_done, rstd_done = sem("stat_done"), sem("var_done"), sem("sd_done"), sem("rstd_done")
        const_in, x_in, ones_set, xt_done = sem("const_in"), sem("x_in"), sem("ones_set"), sem("xt_done")
        gain_ps, gain_set, g_ps, g_set, g_out = (sem("gain_ps"), sem("gain_set"), sem("g_ps"), sem("g_set"),
                                                 sem("g_out"))
        identb_in = sem("identb_in")
        fin_x, fin_ps, fin_sb = sem("fin_x"), sem("fin_ps"), sem("fin_sb")
        kiw_out, kv_out, y_out = sem("kiw_out"), sem("kv_out"), sem("y_out")
        carried = sem("carried")
        dve_step, act_step = sem("dve_step"), sem("act_step")
        MS = {L: {k: sem(k + L) for k in (
            "mix_in", "strip_in", "kiw_ps", "kiw_sb", "rep_ps", "wbl_set", "qis_set", "kist_in0", "kist_in1",
            "kict_ps", "kic_set", "dots_ps", "r_set", "r_usedS", "r_usedP", "s_evac", "kvt_ps", "kvt_sb",
            "vnew_ps", "vnew_sb", "qbd_set", "pmask_set", "maskS_set", "selb_in", "strip_set", "qk_ps", "nm_set", "p_set", "pt_ps",
            "pt_evac", "pv_ps", "es_in", "es_set", "o_evac", "ot_ps", "ot_evac", "kv_in0", "kv_in1", "ktS_ps",
            "ktS_evac", "qkS_ps", "nmS_set", "psS_set", "ptS_ps", "ptS_evac", "pvS_ps", "esS_in", "esS_set",
            "osS_set", "otS_ps", "otS_evac", "cm_used")} for L in "AB"}

        def used(n):
            return n + 1 + RING

        def over(name):
            n = dict(ffn=GU_CHUNKS + DN_CHUNKS, inA=A_CHUNKS, inB=B_CHUNKS, out=ND)
            return used(at[name][0] + n[name if name in n else name[:3]] - 1)

        def gh_base(name):
            return NF * int(name[3]) + 1

        norm_of = {0: 0, 1: 4, 2: 1, 3: 2, 4: 5, 5: 3}
        STAT = PS[3]

        def halves(ap):
            return ap.rearrange("p (h t) -> p h t", h=2)

        def gain(n, d):
            return gains[:, n * ND + d:n * ND + d + 1]

        def acc(k):
            return PS[k % RING][:, :, 0:HALF]

        block = ctx.enter_context(nc.Block())

        @block.sync
        def _(sp):
            def chunk(n, i, per, parts):
                s = n % RING
                sp.wait_ge(w_split, n + 1 + per * i)
                for dst, src in parts(WST[s]):
                    sp.dma_start(dst, src).then_inc(stage_in[s], 16)

            def cols(w, c0, width=P):
                v = w.rearrange("(b p) n -> p b n", p=P)

                def parts(st):
                    d = st[:, 0:ND * width].rearrange("p (b c) -> p b c", b=ND)
                    return [(d[h * 64:h * 64 + 64], v[h * 64:h * 64 + 64, :, bass.ds(c0, width)]) for h in range(2)]
                return parts

            def cols_of_group(w, g):
                v = w.rearrange("(b p) n -> p b n", p=P)

                def parts(st):
                    d = st[:, :].rearrange("p (b n c) -> p b n c", b=ND, n=KVH)
                    return [(d[:, :, n], v[:, :, (n * GRP + g) * HD:(n * GRP + g + 1) * HD]) for n in range(KVH)]
                return parts

            def ffn(name, l, s):
                n0 = at[name][0]
                wg, wu, wd = io["ffn_w_gate"][l, s], io["ffn_w_up"][l, s], io["ffn_w_down"][l, s]
                with sp.Fori(0, NF // RING) as i:
                    for j in range(2 * RING):
                        chunk(n0 + j, i, 2 * RING, cols((wg, wu)[j % 2], (i * RING + j // 2) * P))
                v = wd.rearrange("(q b p) n -> q p b n", q=RING, p=P)
                with sp.Fori(0, ND) as i:
                    for q in range(RING):
                        def parts(st):
                            d = st[:, 0:DB * P].rearrange("p (b c) -> p b c", b=DB)
                            return [(d[h * 64:h * 64 + 64], v[q, h * 64:h * 64 + 64, :, bass.ds(i * P, P)])
                                    for h in range(2)]
                        chunk(n0 + GU_CHUNKS + q, i, RING, parts)

            def project_out(name, w, first, last):
                n0 = at[name][0]
                v = w.rearrange("(n g d) m -> n d g m", n=KVH, d=HD)
                for t in range(first, last):
                    def parts(st):
                        d = st[:, :].rearrange("p (g c) -> p g c", g=GRP)
                        return [(d[n * HD:(n + 1) * HD], v[n, :, :, t * P:(t + 1) * P]) for n in range(KVH)]
                    chunk(n0 + t, 0, 0, parts)

            def kist(b):
                ms = MS["A"]
                if b < 2:
                    sp.wait_ge(w_used, over("ffn0"))
                else:
                    sp.wait_ge(ms["kict_ps"], 2 * (b - 1))
                with sp.Fori(0, NPG) as j:
                    page = sp.value_load(io["page_table"][b:b + 1, bass.ds(j, 1)], min_val=0, max_val=NPOOL - 1)
                    sp.dma_start(mixers["A"]["kist"][:, b % 2, bass.ds(j, 1), :],
                                 io["cache_idx"][0, bass.ds(page, 1)].rearrange("a k d -> k a d"))\
                      .then_inc(ms[f"kist_in{b % 2}"], 16)

            def kv_pages(b):
                ms = MS["A"]
                if b == 0:
                    sp.wait_ge(ms["pmask_set"], NQT - 1)
                elif b == 1:
                    sp.wait_ge(ms["ot_evac"], 2 * NQT)
                else:
                    sp.wait_ge(ms["pvS_ps"], b - 1)
                with sp.Fori(0, NPG) as j:
                    page = sp.value_load(io["page_table"][b:b + 1, bass.ds(j, 1)], min_val=0, max_val=NPOOL - 1)
                    sp.dma_start(mixers["A"][f"kv{b % 2}"][:, bass.ds(j, 1), :],
                                 io["cache_kv"][0, bass.ds(page, 1)].rearrange("a k s n d -> k a (s n d)"))\
                      .then_inc(ms[f"kv_in{b % 2}"], 16)

            ffn("ffn0", 0, 0)
            w = io["a_w_in"][0]
            n0 = at["inA"][0]
            o_qi = QW + 2 * KVW
            todo = [cols(w, o_qi + IH * IDIM, IDIM + IH)] + [cols(w, o_qi + c * P) for c in range(IH // 2)]
            todo += [cols(w, QW), cols(w, QW + KVW)] + [cols_of_group(w, g) for g in range(GRP)]
            for c, parts in enumerate(todo):
                chunk(n0 + c, 0, 0, parts)
                if 2 <= c < 6:
                    kist(2 * (c - 2))
                    kist(2 * (c - 2) + 1)
            project_out("outA", io["a_w_out"][0], 0, RING)
            for b in range(NB):
                kv_pages(b)
            project_out("outA", io["a_w_out"][0], RING, ND)
            ffn("ffn1", 0, 1)
            ffn("ffn2", 1, 0)
            w = io["b_w_in"][0]
            todo = [cols(w, QW), cols(w, QW + KVW)] + [cols_of_group(w, g) for g in range(GRP)]
            for c, parts in enumerate(todo):
                chunk(at["inB"][0] + c, 0, 0, parts)
            project_out("outB", io["b_w_out"][0], 0, ND)
            ffn("ffn3", 1, 1)

        @block.gpsimd
        def _(pool):
            pool.memset(warm[:, 0:1], 0.0).then_inc(w_split, RING)
            pool.memset(warm[:, 1:2], 0.0).then_inc(w_used, RING)
            pool.memset(warm[:, 2:3], 0.0).then_inc(acc_evac, RING)
            pool.memset(warm[:, 3:4], 0.0).then_inc(gh_ready, 1)
            pool.dma_start(identb[:, :], io["c_ident"]).then_inc(identb_in, 16)

            def split(n, i, per, width):
                s = n % RING
                k = 0 if i is None else per * i
                pool.wait_ge(stage_in[s], 32 * (n // RING + 1) + (0 if i is None else 32 * (per // RING) * i))
                pool.wait_ge(w_used, n + 1 + k)
                if i is not None:
                    pool.sem_inc(carried, 1)
                nc.gpsimd.tensor_copy(WSP[s][:, 0, 0:width], WST[s][:, 0:width]).then_inc(w_hi, 1)
                pool.wait_ge(w_hi, n + 1 + k)
                nc.gpsimd.tensor_tensor(WSP[s][:, 1, 0:width], WST[s][:, 0:width],
                                        WSP[s][:, 0, 0:width].bitcast(F32), ALU.subtract).then_inc(w_split, 1)

            def ffn(name):
                n0 = at[name][0]
                with pool.Fori(0, NF // RING) as i:
                    for j in range(2 * RING):
                        split(n0 + j, i, 2 * RING, ND * P)
                with pool.Fori(0, ND) as i:
                    for q in range(RING):
                        split(n0 + GU_CHUNKS + q, i, RING, DB * P)

            ffn("ffn0")
            pool.wait_ge(w_used, over("ffn0"))
            pool.dma_start(mixers["A"]["selb"][:, :, :], io["c_selb"].rearrange("s (b r) -> s b r", b=NB))\
                .then_inc(MS["A"]["selb_in"], 16)
            for c in range(A_CHUNKS):
                split(at["inA"][0] + c, None, 0, ND * (IDIM + IH) if c == 0 else ND * P)
            for t in range(ND):
                split(at["outA"][0] + t, None, 0, ND * P)
            ffn("ffn1")
            ffn("ffn2")
            for c in range(B_CHUNKS):
                split(at["inB"][0] + c, None, 0, ND * P)
            for t in range(ND):
                split(at["outB"][0] + t, None, 0, ND * P)
            ffn("ffn3")

        @block.tensor
        def _(pe):
            mm = nc.tensor.matmul

            def mm3(out, slot, b, width, H, L, first, last):
                w = WSP[slot]
                for k, (part, x) in enumerate(((0, H), (0, L), (1, H))):
                    for h in range(2):
                        ins = mm(out[0:width, h, :], w[:, part, b * width:(b + 1) * width],
                                 x[:, h * HALF:(h + 1) * HALF], start=first and k == 0, stop=last and k == 2)
                return ins

            def statistics(e):
                pe.wait_ge(ssum_done, 8 * e + 8)
                for h in range(2):
                    ins = mm(STAT[:, h, 0:HALF], ones[:, :], ssum[:, h * HALF:(h + 1) * HALF], start=True, stop=True)
                ins.then_inc(stat_done, 1)

            def project(n, a, i, per, width):
                k = 0 if i is None else per * i
                pe.wait_ge(w_split, n + 1 + RING + k)
                pe.wait_ge(acc_evac, a + 1 + k)
                for b in range(ND):
                    ins = mm3(acc(a), n % RING, b, width, XH[:, b, :], XL[:, b, :], b == 0, b == ND - 1)
                ins.then_inc(w_used, 1)

            def ffn(name):
                n0, a0, e = at[name]
                pe.wait_ge(xl_done, 8 * e)
                statistics(e - 1)
                with pe.Fori(0, NF // RING) as i:
                    for j in range(2 * RING):
                        project(n0 + j, a0 + j, i, 2 * RING, P)
                aend = a0 + GU_CHUNKS
                pe.wait_ge(acc_evac, aend - 1 + RING)
                with pe.Fori(0, ND // 2) as i:
                    for j in range(2):
                        pe.wait_ge(x_upd, 8 * e + j - 1 + 2 * i)
                        for q in range(RING):
                            n = n0 + GU_CHUNKS + j * RING + q
                            pe.wait_ge(w_split, n + 1 + RING + 2 * RING * i)
                            pe.wait_ge(gh_ready, gh_base(name) + DB * (q + 1))
                            for b in range(DB):
                                ins = mm3(acc(aend + j), n % RING, b, P, GH[:, q * DB + b, :], GL[:, q * DB + b, :],
                                          q == 0 and b == 0, q == RING - 1 and b == DB - 1)
                            ins.then_inc(w_used, 1)

            def project_out(name, aend):
                n0, _, e = at[name]
                for t in range(ND):
                    n = n0 + t
                    if t > 1:
                        pe.wait_ge(x_upd, 8 * e + t - 1)
                    pe.wait_ge(w_split, n + 1 + RING)
                    for b in range(ND):
                        ins = mm3(acc(aend + t % 2), n % RING, b, P, XH[:, b, :], XL[:, b, :], b == 0, b == ND - 1)
                    ins.then_inc(w_used, 1)

            def mixer_new_rows(m, ms, a, first_bank):
                pe.wait_ge(acc_evac, a + RING)
                for t in range(NTT):
                    w = min(P, TOK - t * P)
                    if t > 1:
                        pe.wait_ge(ms["kvt_sb"], t - 1)
                    bk = bank[6 + t % 2]
                    nc.tensor.transpose(bk[0:w, 0:P], m["kT"][:, t * P:t * P + w], ident[:, :])
                    nc.tensor.transpose(bk[0:w, P:2 * P], m["vT"][:, t * P:t * P + w], ident[:, :])\
                        .then_inc(ms["kvt_ps"], 1)
                for h in range(2):
                    pe.wait_ge(ms["kvt_sb"], NTT - 1 + h)
                    bk = bank[6 + (NTT + h) % 2]
                    for k in range(NB // 2):
                        b = h * NB // 2 + k
                        ins = nc.tensor.transpose(bk[0:NT, k * P:(k + 1) * P],
                                                  m["vT"][:, SEQ + b * NT:SEQ + (b + 1) * NT], ident[:, :])
                    ins.then_inc(ms["vnew_ps"], 1)

            def prompt_attention(L, m, ms, aend):
                units = [(i, g) for i in range(NQT) for g in range(GRP)]
                pe.wait_ge(acc_evac, aend + RING)
                pe.wait_ge(ms["kvt_sb"], NTT)
                pe.wait_ge(ms["vnew_sb"], 2)

                def logits(u):
                    i, g = units[u]
                    k0, nk = key_range(L, i)
                    if u > 1:
                        pe.wait_ge(ms["p_set"], 2 * (u - 1))
                    masked = L == "A" and i > 0
                    if masked:
                        pe.wait_ge(ms["pmask_set"], i)
                        pe.wait_ge(identb_in, 16)
                        for n in range(KVH):
                            mm(PS[u % 2][:, n, 0:nk], identb[:, :], m["pmask"][:, i - 1, 0:nk], start=True, stop=False)
                    for n in range(KVH):
                        h = slice(n * HD, (n + 1) * HD)
                        ins = mm(PS[u % 2][:, n, 0:nk], m["qT"][h, g, i * P:(i + 1) * P], m["kT"][h, k0:k0 + nk],
                                 start=not masked, stop=True)
                    ins.then_inc(ms["qk_ps"], 1)

                logits(0)
                logits(1)
                for u, (i, g) in enumerate(units):
                    k0, nk = key_range(L, i)
                    if g == 0 and i > 0:
                        pe.wait_ge(ms["ot_evac"], 2 * i)
                    for n in range(KVH):
                        pe.wait_ge(ms["p_set"], 2 * u + n + 1)
                        if u > 0:
                            pe.wait_ge(ms["pt_evac"], 2 * u - 1 + n)
                        for k in range(nk // P):
                            ins = nc.tensor.transpose(bank[4 + n][:, k * P:(k + 1) * P],
                                                      m["p"][:, u % 2, n, k * P:(k + 1) * P], ident[:, :])
                        ins.then_inc(ms["pt_ps"], 1)
                    if u + 2 < len(units):
                        logits(u + 2)
                    for n in range(KVH):
                        pe.wait_ge(ms["pt_evac"], 2 * u + n + 1)
                        if g == 0 and i > 0:
                            pe.wait_ge(ms["o_evac"], 2 * i)
                        for k in range(nk // P):
                            ins = mm(bank[6 + n][:, g * HD:(g + 1) * HD], m["pt"][:, n, k, :],
                                     m["kvtok"][:, k0 // P + k, KVW + n * HD:KVW + (n + 1) * HD],
                                     start=k == 0, stop=k == nk // P - 1)
                        ins.then_inc(ms["pv_ps"], 1)
                    if g == GRP - 1:
                        pe.wait_ge(ms["o_evac"], 2 * i + 2)
                        for h in range(2):
                            pe.wait_ge(ms["pt_evac"], 2 * u + 2)
                            for k in range(4):
                                ins = nc.tensor.transpose(bank[4 + h][:, k * P:(k + 1) * P],
                                                          m["otok"][:, 4 * h + k, :, :], ident[:, :])
                            ins.then_inc(ms["ot_ps"], 1)

            def sample_attention(L, m, ms):
                npg, ktg, ptg, ring = sample_shape(L)
                LG = sample_logits
                pe.wait_ge(ms["ot_evac"], 2 * NQT)
                pe.wait_ge(ms["qbd_set"], 1)
                if L == "A":
                    pe.wait_ge(ms["maskS_set"], 1)
                    pe.wait_ge(ms["selb_in"], 16)

                def bank_of(kind, b, k):
                    at_ = ring.index((kind, b, k))
                    if at_ > 1:
                        kind0, b0, k0 = ring[at_ - 2]
                        if kind0 == "kt":
                            pe.wait_ge(ms["ktS_evac"], b0 * len(ktg) + k0 + 1)
                        else:
                            pe.wait_ge(ms["ptS_evac"], b0 * len(ptg) + k0 + 1)
                    return bank[5 + at_ % 2]

                def keys(b):
                    if L == "A":
                        pe.wait_ge(ms[f"kv_in{b % 2}"], 16 * NPG * (b // 2 + 1))
                    else:
                        pe.wait_ge(ms["kv_in0"], 16)
                    for k, pages in enumerate(ktg):
                        bk = bank_of("kt", b, k)
                        for c, j in enumerate(pages):
                            src = m[f"kv{b % 2}"][:, j, 0:KVW] if L == "A" else m["kv"][:, b, 0:KVW]
                            ins = nc.tensor.transpose(bk[:, c * P:(c + 1) * P], src, ident[:, :])
                        ins.then_inc(ms["ktS_ps"], 1)

                def logits(b):
                    pe.wait_ge(ms["ktS_evac"], len(ktg) * (b + 1))
                    if b:
                        pe.wait_ge(ms["psS_set"], b)
                    q = m["qbd"][:, b, :]
                    for c in range(0, npg * PAGE, SEQ):
                        w = min(SEQ, npg * PAGE - c)
                        if L == "A":
                            mm(LG[:, c:c + w], m["selb"][:, b, :], m["maskS"][:, c:c + w], start=True, stop=False)
                        mm(LG[:, c:c + w], q, m["KT"][:, b % 2, c:c + w], start=L == "B", stop=True)
                    c = npg * PAGE
                    if L == "A":
                        mm(LG[:, c:c + NT], m["selb"][:, b, :], m["maskS"][:, c:c + NT], start=True, stop=False)
                    mm(LG[:, c:c + NT], q, m["kT"][:, SEQ + b * NT:SEQ + (b + 1) * NT], start=L == "B", stop=True)\
                        .then_inc(ms["qkS_ps"], 1)

                def weights_transposed(b):
                    pe.wait_ge(ms["psS_set"], b + 1)
                    for k, tiles in enumerate(ptg):
                        bk = bank_of("pt", b, k)
                        for c, j in enumerate(tiles):
                            w = P if j < npg else NT
                            ins = nc.tensor.transpose(bk[0:w, c * P:(c + 1) * P], m["ps"][:, j * P:j * P + w],
                                                      ident[:, :])
                        ins.then_inc(ms["ptS_ps"], 1)

                def values(b):
                    pe.wait_ge(ms["ptS_evac"], len(ptg) * (b + 1))
                    if b:
                        pe.wait_ge(ms["otS_evac"], b)
                    for j in range(npg):
                        v = m[f"kv{b % 2}"][:, j, KVW:2 * KVW] if L == "A" else m["kv"][:, b, KVW:2 * KVW]
                        mm(bank[7][:, 0:P], m["pts"][:, j, :], v, start=j == 0, stop=False)
                    mm(bank[7][:, 0:P], m["pts"][0:NT, npg, :], m["vnew"][:, b, :], start=False, stop=True)\
                        .then_inc(ms["pvS_ps"], 1)

                keys(0)
                logits(0)
                keys(1)
                for b in range(NB):
                    weights_transposed(b)
                    values(b)
                    if b + 1 < NB:
                        logits(b + 1)
                    pe.wait_ge(ms["osS_set"], b + 1)
                    nc.tensor.transpose(bank[7][:, P:2 * P], m["os"][:, :], ident[:, :]).then_inc(ms["otS_ps"], 1)
                    if b + 2 < NB:
                        keys(b + 2)
                pe.wait_ge(ms["otS_evac"], NB)

            def indexer(m, ms, a0):
                u = 0
                pe.wait_ge(ms["qis_set"], 1)
                pe.wait_ge(ms["wbl_set"], 1)
                pe.wait_ge(ms["kic_set"], 2 * NB)
                pe.wait_ge(acc_evac, a0 + 3 + RING)
                groups = [(e, q) for q in range(2) for e in range(2)] + [None]
                todo = [(k, gr, j) for k, gr in enumerate(groups) for j in range(NB // 2)]

                def dots(u, k, gr, j):
                    if u > 1:
                        pe.wait_ge(ms["r_set"], u - 1)
                    else:
                        pe.wait_ge(ms["kic_set"], 2 * NB)
                    for bb in range(2):
                        b = 2 * j + bb
                        e = gr[0] if gr else 0
                        h = slice(e * IDIM, (e + 1) * IDIM)
                        w = SEQ if gr else NT
                        keys = m["kic"][h, b, 4 * gr[1]:4 * gr[1] + 4, :] if gr else \
                            m["kiT"][h, SEQ + b * NT:SEQ + (b + 1) * NT]
                        ins = mm(bank[6 + u % 2][bb * 64:(bb + 1) * 64, 0:w], m["qiS"][h, b, :, :], keys,
                                 start=True, stop=True)
                    ins.then_inc(ms["dots_ps"], 1)

                def weigh(u, k, gr, j):
                    w = SEQ if gr else NT
                    pe.wait_ge(ms["r_set"], u + 1)
                    if j == 0 and k > 1:
                        pe.wait_ge(ms["s_evac"], k - 1)
                    ins = mm(bank[4 + k % 2][0:NS, 0:w], m["wbl"][:, j, :], m["r"][:, u % 2, 0:w],
                             start=j == 0, stop=j == NB // 2 - 1)
                    ins.then_inc(ms["r_usedS"], 1)

                for u, (k, gr, j) in enumerate(todo):
                    dots(u, k, gr, j)
                    if u:
                        weigh(u - 1, *todo[u - 1])
                weigh(u, *todo[u])
                u = len(todo)
                for i in range(1, NQT):
                    for h in range(IH):
                        pe.wait_ge(ms["r_set"], u - 1)
                        s = slice(h % 2 * IDIM, (h % 2 + 1) * IDIM)
                        mm(bank[6 + u % 2][:, 0:(i + 1) * P], m["qiT"][s, h // 2, i * P:(i + 1) * P],
                           m["kiT"][s, 0:(i + 1) * P], start=True, stop=True).then_inc(ms["dots_ps"], 1)
                        u += 1
                pe.wait_ge(ms["r_set"], u)

            pe.wait_ge(const_in, 16 * N_CONST)
            pe.wait_ge(ones_set, 1)
            nc.tensor.transpose(bank[6][:, 0:7 * ND], grows[:, :], ident[0:7 * ND, 0:7 * ND]).then_inc(gain_ps, 1)
            mm(bank[7][0:HEADS, 0:GW], tabx[:, :], coef[:, :], start=True, stop=True).then_inc(g_ps, 1)
            pe.wait_ge(x_in, 16 * NTT)
            for d in range(ND):
                if d > 2:
                    pe.wait_ge(x_upd, d - 2)
                for t in range(NTT):
                    w = min(P, TOK - t * P)
                    ins = nc.tensor.transpose(PS[d % RING][:, t // 4, t % 4 * P:t % 4 * P + w],
                                              xtok[0:w, t, d * P:(d + 1) * P], ident[0:w, 0:w])
                ins.then_inc(xt_done, 1)

            ffn("ffn0")
            m, ms = mixers["A"], MS["A"]
            n0, a0, e = at["inA"]
            pe.wait_ge(xl_done, 8 * e)
            statistics(e - 1)
            pe.wait_ge(rstd_done, e)
            for c in range(1 + IH // 2):
                project(n0 + c, a0 + c, None, 0, IDIM + IH if c == 0 else P)
                if c:
                    for b in (2 * c - 2, 2 * c - 1):
                        pe.wait_ge(ms[f"kist_in{b % 2}"], 16 * NPG * (b // 2 + 1))
                        for h in range(2):
                            if b:
                                pe.wait_ge(ms["kic_set"], 2 * b - 1 + h)
                            for k in range(4):
                                ins = nc.tensor.transpose(
                                    bank[6 + h][:, k * P:(k + 1) * P],
                                    m["kist"][:, b % 2, 8 * h + 2 * k:8 * h + 2 * k + 2, :], ident[:, :])
                            ins.then_inc(ms["kict_ps"], 1)
            pe.wait_ge(ms["kic_set"], 2 * NB)
            for t in range(NTT):
                w = min(P, TOK - t * P)
                nc.tensor.transpose(bank[6][0:w, t * 72:t * 72 + IDIM], m["kiT"][0:IDIM, t * P:t * P + w],
                                    ident[0:IDIM, 0:IDIM])
                ins = nc.tensor.transpose(bank[6][0:w, t * 72 + IDIM:(t + 1) * 72],
                                          sq[IDIM:IDIM + IH, t * P:t * P + w], ident[IDIM:IDIM + IH, IDIM:IDIM + IH])
            ins.then_inc(ms["kiw_ps"], 1)
            pe.wait_ge(ms["mix_in"], 16 * N_MIX["A"])
            mm(bank[7][:, 0:NS], m["rep"][IDIM:IDIM + IH, :], sq[IDIM:IDIM + IH, SEQ:TOK], start=True, stop=True)\
                .then_inc(ms["rep_ps"], 1)
            pe.wait_ge(ms["kiw_sb"], 1)
            indexer(m, ms, a0)
            c = 1 + IH // 2
            pe.wait_ge(ms["s_evac"], 5)
            for c in range(c, c + 3):
                project(n0 + c, a0 + c, None, 0, P)
            mixer_new_rows(m, ms, a0 + c, 6)
            for c in range(c + 1, A_CHUNKS):
                project(n0 + c, a0 + c, None, 0, P)
            aend = a0 + A_CHUNKS
            prompt_attention("A", m, ms, aend)
            sample_attention("A", m, ms)
            project_out("outA", aend)
            ffn("ffn1")
            ffn("ffn2")
            m, ms = mixers["B"], MS["B"]
            n0, a0, e = at["inB"]
            pe.wait_ge(xl_done, 8 * e)
            statistics(e - 1)
            pe.wait_ge(rstd_done, e)
            for c in range(3):
                project(n0 + c, a0 + c, None, 0, P)
            mixer_new_rows(m, ms, a0 + c, 6)
            for c in range(c + 1, B_CHUNKS):
                project(n0 + c, a0 + c, None, 0, P)
            aend = a0 + B_CHUNKS
            prompt_attention("B", m, ms, aend)
            sample_attention("B", m, ms)
            project_out("outB", aend)
            ffn("ffn3")
            pe.wait_ge(x_upd, 8 * 7)
            statistics(6)
            for t in range(NTT):
                w = min(P, TOK - t * P)
                for h in range(2):
                    k = 2 * t + h
                    pe.wait_ge(fin_x, 4 * h + 4)
                    if k > 2:
                        pe.wait_ge(fin_sb, k - 2)
                    for c in range(4):
                        ins = nc.tensor.transpose(PS[k % 3][0:w, 0, c * P:(c + 1) * P], X[:, 4 * h + c, t * P:t * P + w],
                                                  ident[:, :])
                    ins.then_inc(fin_ps, 1)

        @block.scalar
        def _(act):
            fn = nc.scalar.activation
            steps = Steps(act, act_step)

            def update(e, deferred=False):
                def high(d):
                    fn(XH[:, d, :], X[:, d, :], ACT.Copy, scale=gain(norm_of[e], d)).then_inc(xh_done, 1)
                for d in range(ND):
                    act.wait_ge(x_upd, 8 * e + d + 1)
                    if e or d:
                        act.wait_ge(ssum_done, 8 * e + d)
                    fn(sq[:, :], X[:, d, :], ACT.Square).then_inc(sq_done, 1)
                    if e in norm_of and not deferred:
                        high(d)
                if deferred:
                    act.wait_ge(w_used, over({2: "outA", 5: "outB"}[e]))
                    for d in range(ND):
                        high(d)

            def root(e):
                act.wait_ge(var_done, e + 1)
                fn(rstd[:, :], rstd[:, :], ACT.Sqrt).then_inc(sd_done, 1)

            def ffn(name):
                n0, a0, e = at[name]
                root(e - 1)
                with act.Fori(0, NF // RING) as i:
                    for j in range(RING):
                        act.wait_ge(acc_evac, RING + a0 + 2 * j + 1 + 2 * RING * i)
                        fn(gs[:, j % 2, :], gs[:, j % 2, :], ACT.Silu).then_inc(silu_done, 1)

            def copy_rows(m, ms, L):
                for t in range(NTT):
                    w = min(P, TOK - t * P)
                    act.wait_ge(ms["kvt_ps"], t + 1)
                    fn(m["kvtok"][0:w, t, :], bank[6 + t % 2][0:w, 0:2 * KVW], ACT.Copy).then_inc(ms["kvt_sb"], 1)
                for h in range(2):
                    act.wait_ge(ms["vnew_ps"], h + 1)
                    fn(m["vnew"][:, 4 * h:4 * h + 4, :],
                       bank[6 + (NTT + h) % 2][0:NT, :].rearrange("t (b c) -> t b c", b=4), ACT.Copy)\
                        .then_inc(ms["vnew_sb"], 1)
                act.wait_ge(ms["kvt_sb"], NTT)

            def attention_loads(m, ms):
                act.wait_ge(g_out, 16)
                act.dma_start(m["strip"].rearrange("p n g x -> p (n g) x"),
                              bass.AP(tensor=gscr, offset=P - 1, ap=[[SKEW, P], [GW, HEADS], [1, 2 * P]]))\
                    .then_inc(ms["strip_in"], 16)
                for h in range(HEADS):
                    act.dma_start(m["biasS"][h * NT:(h + 1) * NT, :],
                                  bass.AP(tensor=gscr, offset=h * GW + P - 1, ap=[[SKEW, NT], [1, NEAR]]))\
                        .then_inc(ms["strip_in"], 16)

            def prompt_attention(L, m, ms):
                units = [(i, g) for i in range(NQT) for g in range(GRP)]

                def exps(u):
                    i, g = units[u]
                    nk = key_range(L, i)[1]
                    act.wait_ge(ms["nm_set"], u + 1)
                    if u > 1:
                        act.wait_ge(ms["pt_ps"], 2 * (u - 1))
                    for n in range(KVH):
                        fn(m["p"][:, u % 2, n, 0:nk], PS[u % 2][:, n, 0:nk], ACT.Exp,
                           bias=m["nm"][:, i, n, g:g + 1], accum_out=m["rs"][:, i, n, g:g + 1])\
                            .then_inc(ms["p_set"], 1)

                exps(0)
                for u, (i, g) in enumerate(units):
                    if u + 1 < len(units):
                        exps(u + 1)
                    nk = key_range(L, i)[1]
                    for n in range(KVH):
                        act.wait_ge(ms["pt_ps"], 2 * u + n + 1)
                        if u:
                            act.wait_ge(ms["pv_ps"], 2 * u - 1 + n)
                        fn(m["pt"][:, n, 0:nk // P, :].rearrange("p a b -> p (a b)"), bank[4 + n][:, 0:nk], ACT.Copy)\
                            .then_inc(ms["pt_evac"], 1)
                    if L == "B" and g == GRP - 1:
                        act.wait_ge(ms["es_in"], i + 1)
                        fn(m["es"][:, :, :], m["es"][:, :, :], ACT.Exp).then_inc(ms["es_set"], 1)

            def sample_attention(L, m, ms):
                npg, ktg, ptg, ring = sample_shape(L)

                def keys(b):
                    for k, pages in enumerate(ktg):
                        act.wait_ge(ms["ktS_ps"], b * len(ktg) + k + 1)
                        if b > 1:
                            act.wait_ge(ms["qkS_ps"], b - 1)
                        w = len(pages) * P
                        fn(m["KT"][:, b % 2, pages[0] * P:pages[0] * P + w],
                           bank[5 + ring.index(("kt", b, k)) % 2][:, 0:w], ACT.Copy).then_inc(ms["ktS_evac"], 1)

                keys(0)
                keys(1)
                for b in range(NB):
                    act.wait_ge(ms["nmS_set"], b + 1)
                    if b:
                        act.wait_ge(ms["ptS_ps"], len(ptg) * b)
                    fn(m["ps"][:, 0:npg * PAGE + NT], sample_logits[:, 0:npg * PAGE + NT], ACT.Exp,
                       bias=m["nmS"][:, b:b + 1], accum_out=m["rsS"][:, b:b + 1]).then_inc(ms["psS_set"], 1)
                    if L == "B":
                        fn(m["esS"][:, b:b + 1], m["nsinkS"][:, :], ACT.Exp, scale=-1.0,
                           bias=m["nmS"][:, b:b + 1]).then_inc(ms["esS_set"], 1)
                    if b + 2 < NB:
                        keys(b + 2)

            for dst, src in ((ident[:, :], io["c_ident"]), (grows[0:4 * ND, :], io["ffn_norm"].rearrange(
                    "l s (d p) -> (l s d) p", p=P)), (grows[4 * ND:6 * ND, :], io["mix_norm"].rearrange(
                    "l (d p) -> (l d) p", p=P)), (grows[6 * ND:7 * ND, :], io["final_norm"].rearrange(
                    "(d p) -> d p", p=P)), (tabx[0:NBUCK, :], io["rel_bias"]), (coef[:, :], io["c_coef"])):
                act.dma_start(dst, src).then_inc(const_in, 16)
            for t in range(NTT):
                src = io["x_prompt"][0, t * P:(t + 1) * P, :] if t < NQT else \
                    io["x_sample"].rearrange("b t d -> (b t) d")
                act.dma_start(xtok[0:src.shape[0], t, :], src).then_inc(x_in, 16)
            act.wait_ge(gain_ps, 1)
            fn(gains[:, :], bank[6][:, 0:7 * ND], ACT.Copy).then_inc(gain_set, 1)
            act.wait_ge(g_ps, 1)
            fn(gvec[:, :], bank[7][0:HEADS, 0:GW], ACT.Copy).then_inc(g_set, 1)
            act.wait_ge(g_set, 1)
            act.dma_start(bass.AP(tensor=gscr, offset=0, ap=[[GW, HEADS], [SKEW + 1, P], [1, GW]]),
                          gvec[:, :].unsqueeze(1).to_broadcast([HEADS, P, GW])).then_inc(g_out, 16)
            act.wait_ge(gain_set, 1)
            update(0)
            act.wait_ge(g_out, 16)
            ffn("ffn0")
            update(1)
            m, ms = mixers["A"], MS["A"]
            act.wait_ge(w_used, over("ffn0"))
            act.wait_ge(gh_ready, gh_base("ffn1"))
            for name, key in (("pairm", "c_pairm"), ("cmask", "c_cmask"), ("rep", "c_rep"), ("tailm", "c_tailm")):
                dst = m[name]
                dst = dst.rearrange("p a b -> p (a b)") if name == "pairm" else dst[:, :]
                act.dma_start(dst, io[key]).then_inc(ms["mix_in"], 16)
            root(1)
            for b in range(NB):
                for h in range(2):
                    act.wait_ge(ms["kict_ps"], 2 * b + h + 1)
                    fn(m["kic"][:, b, 4 * h:4 * h + 4, :].rearrange("p a b -> p (a b)"), bank[6 + h][:, :], ACT.Copy)\
                        .then_inc(ms["kic_set"], 1)
            act.wait_ge(ms["kiw_ps"], 1)
            kw = IDIM + IH
            fn(m["kiw"][:, 0:NQT, :].rearrange("p a b -> p (a b)"), bank[6][:, 0:NQT * kw], ACT.Copy)
            fn(m["kiw"][0:NS, NQT, :], bank[6][0:NS, NQT * kw:NTT * kw], ACT.Copy).then_inc(ms["kiw_sb"], 1)
            act.wait_ge(ms["kiw_sb"], 1)
            act.dma_start(io["new_idx_prompt"][0, 0].rearrange("(t p) d -> p t d", p=P),
                          m["kiw"][:, 0:NQT, 0:IDIM]).then_inc(kiw_out, 16)
            act.dma_start(io["new_idx_sample"][0].rearrange("b t d -> (b t) d"), m["kiw"][0:NS, NQT, 0:IDIM])\
                .then_inc(kiw_out, 16)
            nS = 5 * NB // 2
            for u in range(nS + (NQT - 1) * IH):
                act.wait_ge(ms["dots_ps"], u + 1)
                if 1 < u < nS + 2:
                    act.wait_ge(ms["r_usedS"], u - 1)
                elif u >= nS + 2:
                    act.wait_ge(ms["r_usedP"], u - nS - 1)
                w = (NT if u >= nS - NB // 2 else SEQ) if u < nS else ((u - nS) // IH + 2) * P
                fn(m["r"][:, u % 2, 0:w], bank[6 + u % 2][:, 0:w], ACT.Relu, scale=IDIM ** -0.5)\
                    .then_inc(ms["r_set"], 1)
            copy_rows(m, ms, "A")
            act.dma_start(io["new_kv_prompt"][0, 0].rearrange("(t p) s n d -> p t (s n d)", p=P),
                          m["kvtok"][:, 0:NQT, :]).then_inc(kv_out, 16)
            act.dma_start(io["new_kv_sample"][0].rearrange("b t s n d -> (b t) (s n d)"), m["kvtok"][0:NS, NQT, :])\
                .then_inc(kv_out, 16)
            act.wait_ge(ms["r_usedP"], (NQT - 1) * IH)
            act.wait_ge(ms["cm_used"], NQT - 1)
            act.wait_ge(kiw_out, 32)
            attention_loads(m, ms)
            prompt_attention("A", m, ms)
            sample_attention("A", m, ms)
            act.wait_ge(kv_out, 32)
            update(2, deferred=True)
            ffn("ffn1")
            update(3)
            ffn("ffn2")
            update(4)
            m, ms = mixers["B"], MS["B"]
            act.wait_ge(w_used, over("ffn2"))
            act.wait_ge(gh_ready, gh_base("ffn3"))
            act.dma_start(m["kv"][:, :, :], io["state_win_kv"][0].rearrange("b k s n d -> k b (s n d)"))\
                .then_inc(ms["kv_in0"], 16)
            act.dma_start(io["new_win_sample"][0, :, 0:P - NT].rearrange("b k s n d -> b (k s n d)"),
                          io["state_win_kv"][0, :, NT:P].rearrange("b k s n d -> b (k s n d)")).then_inc(kv_out, 16)
            sinks, last = io["b_sinks"][0], io["rel_bias"][NBUCK - 1]
            for dst, src in ((m["wm"][:, :], io["c_wmask"]), (m["wmS"][:, :], io["c_wmaskS"])):
                act.dma_start(dst, src).then_inc(ms["mix_in"], 16)
            with nc.allow_non_contiguous_dma(reason="16 numbers, spread over the rows of the heads"):
                for row, wide, tall in ((sinks, m["nsink"], m["nsinkS"][:, :]), (last, m["es"], m["esS"][:, 0:1])):
                    act.dma_start(wide.rearrange("p n g -> p (n g)"),
                                  bass.AP(tensor=row.tensor, offset=row.offset, ap=[[0, P], [1, HEADS]]))\
                        .then_inc(ms["mix_in"], 16)
                    act.dma_start(tall, bass.AP(tensor=row.tensor, offset=row.offset,
                                                ap=[[1, HEADS], [0, NT], [1, 1]])).then_inc(ms["mix_in"], 16)
            attention_loads(m, ms)
            root(4)
            copy_rows(m, ms, "B")
            act.dma_start(io["new_win_prompt"][0, 0].rearrange("k s n d -> k (s n d)"), m["kvtok"][:, NQT - 1, :])\
                .then_inc(kv_out, 16)
            act.dma_start(io["new_win_sample"][0, :, P - NT:P].rearrange("b k s n d -> b k (s n d)"),
                          m["kvtok"][0:NS, NQT, :]).then_inc(kv_out, 16)
            prompt_attention("B", m, ms)
            sample_attention("B", m, ms)
            act.wait_ge(kv_out, 16 * 5)
            update(5, deferred=True)
            ffn("ffn3")
            update(6)
            root(6)
            for t in range(NTT):
                w = min(P, TOK - t * P)
                for h in range(2):
                    k = 2 * t + h
                    act.wait_ge(fin_ps, k + 1)
                    fn(xtok[0:w, t, h * SEQ:(h + 1) * SEQ], PS[k % 3][0:w, 0, :], ACT.Copy).then_inc(fin_sb, 1)
                act.wait_ge(fin_sb, 2 * t + 2)
                dst = io["y_prompt"][0, t * P:(t + 1) * P, :] if t < NQT else \
                    io["y_sample"].rearrange("b t d -> (b t) d")
                act.dma_start(dst, xtok[0:w, t, :]).then_inc(y_out, 16)
            act.wait_ge(y_out, 16 * NTT)

        @block.vector
        def _(dve):
            tt, stt, ts = nc.vector.tensor_tensor, nc.vector.scalar_tensor_tensor, nc.vector.tensor_scalar
            steps = Steps(dve, dve_step)

            def update(e, scale=1.0, aend=0, used_at=None, deferred=False):
                def low(d):
                    dve.wait_ge(xh_done, 8 * e + d + 1)
                    stt(XL[:, d, :], X[:, d, :], gain(norm_of[e], d), XH[:, d, :].bitcast(F32), ALU.mult, ALU.subtract)\
                        .then_inc(xl_done, 1)

                def rest(d):
                    dve.wait_ge(sq_done, 8 * e + d + 1)
                    if d == 0:
                        nc.vector.tensor_copy(ssum[:, :], sq[:, :]).then_inc(ssum_done, 1)
                    else:
                        dve.wait_ge(ssum_done, 8 * e + d)
                        tt(ssum[:, :], ssum[:, :], sq[:, :], ALU.add).then_inc(ssum_done, 1)
                    if e in norm_of and not deferred:
                        low(d)

                for d in range(ND):
                    if e == 0:
                        dve.wait_ge(xt_done, d + 1)
                        nc.vector.tensor_copy(X[:, d, 0:SEQ], PS[d % RING][:, 0, :])
                        nc.vector.tensor_copy(X[:, d, SEQ:TOK], PS[d % RING][:, 1, 0:NS]).then_inc(x_upd, 1)
                    else:
                        dve.wait_ge(w_used, used_at(d))
                        stt(halves(X[:, d, :]), acc(aend + d % 2), scale, halves(X[:, d, :]), ALU.mult, ALU.add)\
                            .then_inc(x_upd, 1)
                    rest(d)
                if deferred:
                    for d in range(ND):
                        low(d)

            def rms(e):
                dve.wait_ge(stat_done, e + 1)
                ts(halves(rstd[:, :]), STAT[:, :, 0:HALF], 1.0 / D, EPS, ALU.mult, ALU.add).then_inc(var_done, 1)
                dve.wait_ge(sd_done, e + 1)
                nc.vector.reciprocal(rstd[:, :], rstd[:, :]).then_inc(rstd_done, 1)
                dve.wait_ge(rstd_done, e + 1)

            def ffn(name):
                n0, a0, e = at[name]
                rms(e - 1)
                with dve.Fori(0, NF // RING) as i:
                    steps.loop(i, 2 * RING)
                    for j in range(RING):
                        k = 2 * RING * i
                        a, n = a0 + 2 * j, n0 + 2 * j
                        g = gs[:, j % 2, :]
                        dve.wait_ge(w_used, used(n) + k)
                        tt(halves(g), acc(a), halves(rstd[:, :]), ALU.mult).then_inc(acc_evac, 1)
                        dve.wait_ge(w_used, used(n + 1) + k)
                        dve.wait_ge(gh_ready, gh_base(name) + j + RING * i)
                        tt(halves(us[:, :]), acc(a + 1), halves(rstd[:, :]), ALU.mult).then_inc(acc_evac, 1)
                        dve.wait_ge(acc_evac, RING + a + 2 + k)
                        dve.wait_ge(silu_done, gh_base(name) + j + RING * i)
                        steps.done(tt(us[:, :], us[:, :], g, ALU.mult))
                        f = bass.ds(i * RING + j, 1)
                        steps.done(nc.vector.tensor_copy(GH[:, f, :].rearrange("p a t -> p (a t)"), us[:, :]))
                        tt(GL[:, f, :].rearrange("p a t -> p (a t)"), us[:, :],
                           GH[:, f, :].rearrange("p a t -> p (a t)").bitcast(F32), ALU.subtract).then_inc(gh_ready, 1)
                steps.end(NF // RING)
                dve.wait_ge(gh_ready, gh_base(name) + NF)
                update(e, 0.5, a0 + GU_CHUNKS, lambda d: used(n0 + GU_CHUNKS + RING * d + RING - 1))

            def project(n, a, outs):
                dve.wait_ge(w_used, used(n))
                for k, (rows, dst, factor) in enumerate(outs):
                    src, r = acc(a)[rows], halves(rstd[rows, :])
                    if factor == 1.0:
                        ins = tt(halves(dst), src, r, ALU.mult)
                    else:
                        ins = stt(halves(dst), src, factor, r, ALU.mult, ALU.mult)
                ins.then_inc(acc_evac, 1)

            def block_diagonal(m, ms, aend):
                steps.done(nc.vector.memset(m["qbd"][:, :, :], 0.0))
                dve.wait_ge(acc_evac, aend + RING)
                for n in range(KVH):
                    h = slice(n * HD, (n + 1) * HD)
                    dst = m["qbd"][h].rearrange("p b (n g t) -> p n g b t", n=KVH, g=GRP)[:, n]
                    ins = nc.vector.tensor_copy(dst, m["qT"][h, :, SEQ:TOK].rearrange("p g (b t) -> p g b t", b=NB))
                ins.then_inc(ms["qbd_set"], 1)

            def select(scores, mask, done):
                ts(mask, scores, TAKEN / 2, MASK, ALU.is_gt, ALU.mult).then_inc(done, 1)

            def top8(scores, mx8):
                steps.done(nc.vector.max(mx8, scores))
                if steps.i is not None:
                    dve.sem_inc(carried, 1)
                steps.done(nc.vector.match_replace(scores, mx8, scores, TAKEN))

            def prompt_attention(L, m, ms, between):
                units = [(i, g) for i in range(NQT) for g in range(GRP)]

                def finish(i):
                    dve.wait_ge(ms["p_set"], 2 * GRP * (i + 1))
                    rs, ri = m["rs"][:, i], m["ri"][:, i]
                    if L == "B":
                        dve.wait_ge(ms["es_set"], i + 1)
                        steps.done(tt(rs, rs, m["es"][:, :, :], ALU.add))
                    steps.done(nc.vector.reciprocal(ri, rs))
                    dve.wait_ge(ms["pv_ps"], 2 * GRP * (i + 1))
                    for n in range(KVH):
                        tt(m["otok"][:, :, n, :], bank[6 + n].rearrange("p (g d) -> p g d", g=GRP),
                           m["ri"][:, i, n, :].unsqueeze(2).to_broadcast([P, GRP, HD]), ALU.mult)\
                            .then_inc(ms["o_evac"], 1)
                    for h in range(2):
                        dve.wait_ge(ms["ot_ps"], 2 * i + h + 1)
                        s = (slice(0, P), slice(4 * h, 4 * h + 4), slice(i * P, (i + 1) * P))
                        src = bank[4 + h].rearrange("p (g t) -> p g t", g=4)
                        steps.done(nc.vector.tensor_copy(XH[s], src))
                        tt(XL[s], src, XH[s].bitcast(F32), ALU.subtract).then_inc(ms["ot_evac"], 1)

                for u, (i, g) in enumerate(units):
                    if g == 0:
                        between(i)
                    k0, nk = key_range(L, i)
                    w = min(nk, 2 * P)
                    dve.wait_ge(ms["qk_ps"], u + 1)
                    near = PS[u % 2][:, :, nk - w:nk]
                    steps.done(tt(near, near, m["strip"][:, :, g, 2 * P - w:2 * P], ALU.add))
                    nm = m["nm"][:, i, :, g]
                    ins = nc.vector.tensor_reduce(nm, PS[u % 2][:, :, 0:nk], AX, ALU.max, negate=True)
                    if L == "B":
                        steps.done(ins)
                        ins = tt(nm, nm, m["nsink"][:, :, g], ALU.min)
                    ins.then_inc(ms["nm_set"], 1)
                    if L == "B" and g == GRP - 1:
                        dve.wait_ge(ms["nm_set"], u + 1)
                        if i:
                            dve.wait_ge(ms["es_set"], i)
                        tt(m["es"][:, :, :], m["nm"][:, i], m["nsink"][:, :, :], ALU.subtract).then_inc(ms["es_in"], 1)
                    if g == 1 and i:
                        finish(i - 1)
                finish(NQT - 1)

            def sample_attention(L, m, ms):
                npg, ktg, ptg, ring = sample_shape(L)
                nk = npg * PAGE + NT
                LG = sample_logits

                def maxima(b):
                    dve.wait_ge(ms["qkS_ps"], b + 1)
                    steps.done(tt(LG[:, nk - NEAR:nk], LG[:, nk - NEAR:nk], m["biasS"][:, :], ALU.add))
                    nm = m["nmS"][:, b:b + 1]
                    ins = nc.vector.tensor_reduce(nm, LG[:, 0:nk], AX, ALU.max, negate=True)
                    if L == "B":
                        steps.done(ins)
                        ins = tt(nm, nm, m["nsinkS"][:, :], ALU.min)
                    ins.then_inc(ms["nmS_set"], 1)

                maxima(0)
                for b in range(NB):
                    if b:
                        dve.wait_ge(ms["pvS_ps"], b)
                    for k, tiles in enumerate(ptg):
                        dve.wait_ge(ms["ptS_ps"], b * len(ptg) + k + 1)
                        bk = bank[5 + ring.index(("pt", b, k)) % 2]
                        full = [j for j in tiles if j < npg]
                        if full:
                            ins = nc.vector.tensor_copy(m["pts"][:, full[0]:full[-1] + 1, :],
                                                        bk[:, 0:len(full) * P].rearrange("p (a b) -> p a b", b=P))
                        if len(full) < len(tiles):
                            c = len(full) * P
                            ins = nc.vector.tensor_copy(m["pts"][0:NT, npg, :], bk[0:NT, c:c + P])
                        ins.then_inc(ms["ptS_evac"], 1)
                    rs, ri = m["rsS"][:, b:b + 1], m["riS"][:, b:b + 1]
                    if L == "B":
                        dve.wait_ge(ms["esS_set"], b + 1)
                        steps.done(tt(rs, rs, m["esS"][:, b:b + 1], ALU.add))
                    steps.done(nc.vector.reciprocal(ri, rs))
                    dve.wait_ge(ms["pvS_ps"], b + 1)
                    ts(m["os"][:, :], bank[7][:, 0:P], ri, None, ALU.mult).then_inc(ms["osS_set"], 1)
                    if b + 1 < NB:
                        maxima(b + 1)
                    dve.wait_ge(ms["otS_ps"], b + 1)
                    part = []
                    for n in range(KVH):
                        h = slice(n * HD, (n + 1) * HD)
                        part.append((bank[7][h, P + n * HD:P + (n + 1) * HD].rearrange("p (g t) -> p g t", g=GRP),
                                     (h, slice(0, GRP), slice(SEQ + b * NT, SEQ + (b + 1) * NT))))
                    for src, s in part:
                        steps.mark(nc.vector.tensor_copy(XH[s], src))
                    steps.settle()
                    for src, s in part:
                        ins = tt(XL[s], src, XH[s].bitcast(F32), ALU.subtract)
                    ins.then_inc(ms["otS_evac"], 1)

            nc.vector.memset(tabx[NBUCK:NBUCK + 1, :], MASK)
            nc.vector.memset(ones[:, :], 1.0).then_inc(ones_set, 1)
            dve.wait_ge(gain_set, 1)
            update(0)
            ffn("ffn0")
            m, ms = mixers["A"], MS["A"]
            n0, a0, e = at["inA"]
            rms(e - 1)
            lo, hi, both = slice(0, IDIM), slice(IDIM, 2 * IDIM), slice(0, P)
            wi = slice(IDIM, IDIM + IH)
            project(n0, a0, [(lo, m["kiT"][lo, :], 1.0), (lo, m["kiT"][hi, :], 1.0), (wi, sq[wi, :], 1.0)])
            for c in range(IH // 2):
                project(n0 + 1 + c, a0 + 1 + c, [(both, m["qiT"][:, c, :], 1.0)])
            dve.wait_ge(acc_evac, a0 + 1 + IH // 2 + RING)
            for src in range(2):
                for dst in range(2):
                    s, d = slice(src * 64, src * 64 + 64), slice(dst * 64, dst * 64 + 64)
                    for c in range(IH // 2):
                        ins = nc.vector.tensor_copy(m["qiS"][d, :, 2 * c + src, :],
                                                    m["qiT"][s, c, SEQ:TOK].rearrange("p (b t) -> p b t", b=NB))
            ins.then_inc(ms["qis_set"], 1)
            dve.wait_ge(ms["rep_ps"], 1)
            dve.wait_ge(ms["mix_in"], 16 * N_MIX["A"])
            for j in range(NB // 2):
                ins = tt(m["wbl"][:, j, :], bank[7][:, 0:NS], m["pairm"][:, j, :], ALU.mult)
            ins.then_inc(ms["wbl_set"], 1)
            dve.wait_ge(ms["kiw_sb"], 1)
            steps.done(ts(m["wis"][:, :, :], m["kiw"][:, 0:NQT, IDIM:IDIM + IH], IH ** -0.5, None, ALU.mult))
            scs = m["scs"]
            pages = scs[:, 0:PAST].rearrange("s (r e c) -> s r e c", e=2, c=PAGE)
            for k in range(5):
                dve.wait_ge(ms["r_usedS"], (k + 1) * NB // 2)
                bk = bank[4 + k % 2]
                if k < 4:
                    nc.vector.tensor_copy(pages[:, 4 * (k // 2):4 * (k // 2) + 4, k % 2, :],
                                          bk[0:NS, :].rearrange("s (r c) -> s r c", r=4)).then_inc(ms["s_evac"], 1)
                else:
                    tt(scs[:, PAST:KEYS], bk[0:NS, 0:NT], m["tailm"][:, :], ALU.add).then_inc(ms["s_evac"], 1)
            k = 0
            for i in range(1, NQT):
                s = m["scp"][:, i - 1, 0:(i + 1) * P]
                for h in range(IH):
                    dve.wait_ge(ms["r_set"], 5 * NB // 2 + k + 1)
                    r, w = m["r"][:, k % 2, 0:(i + 1) * P], m["wis"][:, i, h:h + 1]
                    if h == 0:
                        ins = ts(s, r, w, None, ALU.mult)
                    else:
                        dve.wait_ge(ms["r_usedP"], k)
                        ins = stt(s, r, w, s, ALU.mult, ALU.add)
                    ins.then_inc(ms["r_usedP"], 1)
                    k += 1
                dve.wait_ge(ms["r_usedP"], k)
                diag = m["scp"][:, i - 1, i * P:(i + 1) * P]
                ins = tt(diag, diag, m["cmask"][:, :], ALU.add)
                ins.then_inc(ms["cm_used"], 1)
            dve.wait_ge(ms["cm_used"], NQT - 1)
            c = 1 + IH // 2
            project(n0 + c, a0 + c, [(both, m["kT"][:, :], 1.0)])
            project(n0 + c + 1, a0 + c + 1, [(both, m["vT"][:, :], 1.0)])
            dve.wait_ge(ms["s_evac"], 5)
            rounds = 0
            for g in range(GRP):
                project(n0 + c + 2 + g, a0 + c + 2 + g, [(both, m["qT"][:, g, :], HD ** -0.5)])
                top8(scs[:, :], m["mx8"][0:NS, :])
                rounds += 1
            block_diagonal(m, ms, a0 + A_CHUNKS)

            def prompt_top(i):
                if i == 0:
                    dve.wait_ge(ms["strip_in"], 16 * (1 + HEADS))
                if i + 1 < NQT:
                    s = m["scp"][:, i, 0:(i + 2) * P]
                    with dve.Fori(0, TOPK_P // 8) as k:
                        steps.loop(k, 2)
                        top8(s, m["mx8"][:, :])
                    steps.end(TOPK_P // 8)
                    select(s, m["pmask"][:, i, 0:(i + 2) * P], ms["pmask_set"])

            prompt_attention("A", m, ms, prompt_top)
            with dve.Fori(0, TOPK_S // 8 - rounds) as k:
                steps.loop(k, 2)
                top8(scs[:, :], m["mx8"][0:NS, :])
            steps.end(TOPK_S // 8 - rounds)
            select(scs[:, :], m["maskS"][:, :], ms["maskS_set"])
            sample_attention("A", m, ms)
            n1, _, e = at["outA"]
            update(e, 1.0, a0 + A_CHUNKS, lambda d: used(n1 + d), deferred=True)
            ffn("ffn1")
            ffn("ffn2")
            m, ms = mixers["B"], MS["B"]
            n0, a0, e = at["inB"]
            rms(e - 1)
            project(n0, a0, [(both, m["kT"][:, :], 1.0)])
            project(n0 + 1, a0 + 1, [(both, m["vT"][:, :], 1.0)])
            for g in range(GRP):
                project(n0 + 2 + g, a0 + 2 + g, [(both, m["qT"][:, g, :], HD ** -0.5)])
            block_diagonal(m, ms, a0 + B_CHUNKS)
            dve.wait_ge(ms["mix_in"], 16 * N_MIX["B"])
            dve.wait_ge(ms["strip_in"], 16 * (1 + HEADS))
            steps.mark(tt(m["nsink"][:, :, :], m["es"][:, :, :], m["nsink"][:, :, :], ALU.subtract))
            steps.mark(tt(m["nsinkS"][:, :], m["esS"][:, 0:1], m["nsinkS"][:, :], ALU.subtract))
            steps.mark(tt(m["biasS"][:, :], m["biasS"][:, :], m["wmS"][:, :], ALU.add))
            for n in range(KVH):
                far = m["strip"][:, n, :, 0:P]
                steps.mark(tt(far, far, m["wm"][:, :].unsqueeze(1).to_broadcast([P, GRP, P]), ALU.add))
            steps.settle()
            prompt_attention("B", m, ms, lambda i: None)
            sample_attention("B", m, ms)
            n1, _, e = at["outB"]
            update(e, 1.0, a0 + B_CHUNKS, lambda d: used(n1 + d), deferred=True)
            ffn("ffn3")
            rms(6)
            for d in range(ND):
                stt(X[:, d, :], X[:, d, :], gain(6, d), rstd[:, :], ALU.mult, ALU.mult).then_inc(fin_x, 1)


def key_range(L, i):
    first = 0 if L == "A" else max(0, i - 1) * P
    return first, (i + 1) * P - first


def sample_shape(L):
    npg = NPG if L == "A" else 1
    ktg = [list(range(npg))[k:k + 4] for k in range(0, npg, 4)]
    ptg = [list(range(npg + 1))[k:k + 4] for k in range(0, npg + 1, 4)]
    ring = [("kt", b, k) for b in range(2) for k in range(len(ktg))]
    for b in range(NB):
        ring += [("pt", b, k) for k in range(len(ptg))]
        if b + 2 < NB:
            ring += [("kt", b + 2, k) for k in range(len(ktg))]
    return npg, ktg, ptg, ring


def constants():
    p, c = np.arange(P)[:, None], np.arange(P)[None, :]
    coef = np.zeros((NBUCK + 1, GW), np.float32)
    half = NBUCK // 2
    for m in range(GW):
        n = 2 * P - 1 - m
        if n < 0:
            coef[NBUCK, m] = 1.0
            continue
        log = np.log(np.float32(max(n, 1)) / np.float32(half)) / np.float32(math.log(MAXD / half))
        bucket = n if n < half else min(half + int(log * np.float32(NBUCK - half)), NBUCK - 1)
        coef[bucket, m] += 1.0
        coef[NBUCK - 1, m] -= 1.0
    rep = np.zeros((P, P), np.float32)
    pairm = np.zeros((P, NB // 2, NS), np.float32)
    selb = np.zeros((NS, NB, P), np.float32)
    for bb in range(2):
        for h in range(IH):
            for t in range(NT):
                row = bb * 64 + h * NT + t
                rep[IDIM + h, row] = 1.0
                for j in range(NB // 2):
                    pairm[row, j, (2 * j + bb) * NT + t] = np.float32(IH ** -0.5)
    for b in range(NB):
        for row in range(P):
            selb[b * NT + row % NT, b, row] = 1.0
    ns = np.arange(NS)[:, None]
    return {
        "c_ident": np.eye(P, dtype=np.float32), "c_coef": coef, "c_rep": rep,
        "c_pairm": pairm.reshape(P, -1), "c_selb": selb.reshape(NS, -1),
        "c_cmask": np.where(c > p, MASK, 0.0).astype(np.float32),
        "c_wmask": np.where(c < p, MASK, 0.0).astype(np.float32),
        "c_tailm": np.where(np.arange(NT)[None, :] > ns % NT, MASK, 0.0).astype(np.float32),
        "c_wmaskS": np.where(np.arange(NEAR)[None, :] < p % NT, MASK, 0.0).astype(np.float32),
    }


N_CONST = 6
N_MIX = {"A": 4, "B": 6}
_OUTS = [("y_prompt", (1, SEQ, D)), ("y_sample", (NB, NT, D)), ("new_kv_prompt", (1, 1, SEQ, 2, KVH, HD)),
         ("new_idx_prompt", (1, 1, SEQ, IDIM)), ("new_win_prompt", (1, 1, P, 2, KVH, HD)),
         ("new_kv_sample", (1, NB, NT, 2, KVH, HD)), ("new_idx_sample", (1, NB, NT, IDIM)),
         ("new_win_sample", (1, NB, P, 2, KVH, HD))]


def kernel(**inputs):
    import concourse.bacc as _bacc
    from concourse.bass_utils import run_bass_kernel_spmd as _run

    nc = _bacc.Bacc("TRN2", target_bir_lowering=False, num_devices=1)
    arrays, io = {}, {}
    given = {name: np.ascontiguousarray(a) for name, a in inputs.items()}
    given.update(constants())
    for name, a in given.items():
        arrays[f"in_{name}"] = a
        io[name] = nc.dram_tensor(f"in_{name}", a.shape, mybir.dt.from_np(a.dtype), kind="ExternalInput").ap()
    for name, shape in _OUTS:
        io[name] = nc.dram_tensor(f"out_{name}", shape, F32, kind="ExternalOutput").ap()
    bass_hybrid_step(nc, io)
    r = _run(nc, [arrays], core_ids=[0])
    return tuple(r.results[0][f"out_{name}"] for name, _ in _OUTS)
```

```python
import math
from contextlib import ExitStack

import concourse.bass as bass
import numpy as np
from concourse import mybir

F32 = mybir.dt.float32
F32R = mybir.dt.float32r
BF16 = mybir.dt.bfloat16
ALU = mybir.AluOpType
ACT = mybir.ActivationFunctionType
AX = mybir.AxisListType.X

P = 128
D = 1024
ND = D // P
SEQ = 512
NQT = SEQ // P
NB, NT = 8, 8
NS = NB * NT
TOK = SEQ + NS
HALF = TOK // 2
NTT = -(-TOK // P)
FF = 2688
NF = FF // P
HEADS, HD, KVH = 16, 64, 2
GRP = HEADS // KVH
IH, IDIM = 8, 64
PAST, PAGE = 2048, 128
NPG = PAST // PAGE
NPOOL = 5 * NB * NPG // 4
KEYS = PAST + NT
NEAR = P + NT
TOPK_P = min(256, SEQ // 4)
TOPK_S = min(256, KEYS // 4)
QW, KVW = HEADS * HD, KVH * HD
A_IN = QW + 2 * KVW + IH * IDIM + IDIM + IH
EPS = 1e-6
MASK = -1.0e30
TAKEN = -3.0e38
NBUCK, MAXD = 32, 128
GW = 3 * P

SKEW = HEADS * GW

RING = 3
DB = NF // RING
GU_CHUNKS, DN_CHUNKS = 2 * NF, ND * RING
A_CHUNKS, B_CHUNKS = 1 + IH // 2 + 2 + GRP, 2 + GRP


def layout():
    at, chunk, acc, event = {}, 0, 0, 1
    for name, chunks, accs, events in (
            ("ffn0", GU_CHUNKS + DN_CHUNKS, GU_CHUNKS, 1), ("inA", A_CHUNKS, A_CHUNKS, 0), ("outA", ND, 0, 1),
            ("ffn1", GU_CHUNKS + DN_CHUNKS, GU_CHUNKS, 1), ("ffn2", GU_CHUNKS + DN_CHUNKS, GU_CHUNKS, 1),
            ("inB", B_CHUNKS, B_CHUNKS, 0), ("outB", ND, 0, 1), ("ffn3", GU_CHUNKS + DN_CHUNKS, GU_CHUNKS, 1)):
        at[name] = (chunk, acc, event)
        chunk, acc, event = chunk + chunks, acc + accs, event + events
    return at


class Steps:

    def __init__(self, eng, sem):
        self.eng, self.sem, self.n, self.i, self.per = eng, sem, 0, None, 0

    def mark(self, ins):
        ins.then_inc(self.sem, 1)
        self.n += 1

    def settle(self):
        self.eng.wait_ge(self.sem, self.n if self.i is None else self.i * self.per + self.n)

    def done(self, ins):
        self.mark(ins)
        self.settle()

    def loop(self, i, per):
        self.i, self.per, self.first = i, per, self.n

    def end(self, times):
        assert self.n == self.first + self.per
        self.n, self.i = self.first + self.per * times, None


def mixer_memory(sb, L):
    m = {}

    def mb(c, name, shape, dt=F32):
        m[name] = sb(c, name + L, shape, dt)

    with ExitStack() as c:
        mb(c, "kT", [P, TOK])
        mb(c, "kvtok", [P, NTT, 2 * KVW])
        mb(c, "vnew", [NT, NB, KVW])
        mb(c, "biasS", [P, NEAR])
        mb(c, "nm", [P, NQT, KVH, GRP])
        mb(c, "rs", [P, NQT, KVH, GRP])
        mb(c, "ri", [P, NQT, KVH, GRP])
        mb(c, "es", [P, KVH, GRP])
        mb(c, "nsink", [P, KVH, GRP])
        mb(c, "nmS", [P, NB])
        mb(c, "rsS", [P, NB])
        mb(c, "riS", [P, NB])
        mb(c, "esS", [P, NB])
        mb(c, "nsinkS", [P, 1])
        mb(c, "mx8", [P, 8])
        mb(c, "mx8p", [P, 8])
        if L == "A":
            with ExitStack() as c2:
                mb(c2, "pmask", [P, NQT - 1, SEQ], BF16)
                mb(c2, "scs", [NS, KEYS])
                mb(c2, "kiw", [P, NTT, IDIM + IH])
                mb(c2, "wis", [P, NQT, IH])
                mb(c2, "wbl", [P, NB // 2, NS])
                mb(c2, "pairm", [P, NB // 2, NS])
                mb(c2, "cmask", [P, P])
                mb(c2, "rep", [P, P])
                mb(c2, "tailm", [NS, NT])
            with ExitStack() as c2:
                mb(c2, "kv2", [P, NPG, 2 * KVW])
            mb(c, "kv2room", [P, NPG * 2 * KVW])
            with ExitStack() as c2:
                mb(c2, "kic", [P, NB, NPG // 2, PAGE])
            with ExitStack() as c2:
                mb(c2, "kv0", [P, NPG, 2 * KVW])
                mb(c2, "kv1", [P, NPG, 2 * KVW])
            with ExitStack() as c2:
                mb(c2, "scp", [P, NQT - 1, SEQ])
                mb(c2, "scp_pad", [P, NPG * 2 * KVW - (NQT - 1) * SEQ])
                mb(c2, "p", [P, 2, KVH, SEQ])
                mb(c2, "pt", [P, KVH, NQT, P])
                mb(c2, "otok", [P, GRP, KVH, HD])
            mb(c, "kvroom", [P, 2 * NPG * 2 * KVW])
            mb(c, "maskS", [NS, KEYS], BF16)
            mb(c, "selb", [NS, NB, P], BF16)
            mb(c, "qbd", [P, NB, P])
            with ExitStack() as c2:
                mb(c2, "kist", [P, 2, NPG, IDIM])
            with ExitStack() as c2:
                mb(c2, "qT", [P, GRP, TOK])
                with ExitStack() as c3:
                    mb(c3, "strip", [P, KVH, GRP, 2 * P])
                with ExitStack() as c3:
                    mb(c3, "vT", [P, TOK])
                    mb(c3, "kiT", [P, TOK])
                    mb(c3, "qiT", [P, IH // 2, TOK])
                    mb(c3, "qiS", [P, NB, IH, NT])
                    mb(c3, "r", [P, 2, SEQ])
            with ExitStack() as c2:
                mb(c2, "KT", [P, 2, PAST])
                mb(c2, "ps", [P, KEYS])
                mb(c2, "pts", [P, NPG + 1, P])
                mb(c2, "os", [P, P])
        else:
            mb(c, "kv", [P, NB, 2 * KVW])
            mb(c, "qbd", [P, NB, P])
            mb(c, "wm", [P, P])
            mb(c, "wmS", [P, NEAR])
            mb(c, "qT", [P, GRP, TOK])
            mb(c, "strip", [P, KVH, GRP, 2 * P])
            mb(c, "vT", [P, TOK])
            mb(c, "p", [P, 2, KVH, SEQ])
            mb(c, "pt", [P, KVH, NQT, P])
            mb(c, "otok", [P, GRP, KVH, HD])
            mb(c, "KT", [P, NB, P])
            mb(c, "ps", [P, NB, NEAR])
            mb(c, "pts", [P, NB, P])
            mb(c, "ptsn", [NT, NB, P])
            mb(c, "os", [P, NB, P])
    return m


def bass_hybrid_step(nc, io):
    at = layout()
    ctx = ExitStack()
    with ctx:
        def sb(c, name, shape, dt=F32):
            return c.enter_context(nc.sbuf_tensor(name, shape, dt))

        def sem(name):
            return ctx.enter_context(nc.semaphore(name))

        X = sb(ctx, "X", [P, ND, TOK])
        XH = sb(ctx, "XH", [P, ND, TOK], F32R)
        XL = sb(ctx, "XL", [P, ND, TOK], F32R)
        WST = [sb(ctx, f"WST{s}", [P, ND * P]) for s in range(RING)]
        WSP = [sb(ctx, f"WSP{s}", [P, 2, ND * P], F32R) for s in range(RING)]
        rstd = sb(ctx, "rstd", [P, TOK])
        ssum = sb(ctx, "ssum", [P, TOK])
        sq = sb(ctx, "sq", [P, TOK])
        ident = sb(ctx, "ident", [P, P])
        identb = sb(ctx, "identb", [P, P], BF16)
        ones = sb(ctx, "ones", [P, P])
        gains = sb(ctx, "gains", [P, 7 * ND])
        warm = sb(ctx, "warm", [P, 4])

        with ExitStack() as c:
            GH = sb(c, "GH", [P, NF, TOK], F32R)
            GL = sb(c, "GL", [P, NF, TOK], F32R)
            gs = sb(c, "gs", [P, 2, TOK])
            us = sb(c, "us", [P, TOK])
        with ExitStack() as c:
            xtok = sb(c, "xtok", [P, NTT, D])
            grows = sb(c, "grows", [7 * ND, P])
            tabx = sb(c, "tabx", [NBUCK + 1, HEADS])
            coef = sb(c, "coef", [NBUCK + 1, GW])
            gvec = sb(c, "gvec", [HEADS, GW])

        mixers = {L: mixer_memory(sb, L) for L in "AB"}
        psum = ctx.enter_context(nc.psum_tensor("psum", [P, 8, SEQ], F32))
        bank = [psum[:, k, :] for k in range(8)]
        PS = [psum[:, 2 * k:2 * k + 2, :] for k in range(4)]
        sample_logits = psum[:, 0:5, :].rearrange("p k c -> p (k c)")
        gscr = nc.dram_tensor("gscr", [P * (SKEW + 1)], F32, kind="Internal")
        kscr = nc.dram_tensor("kscr", [NB * NPG, PAGE * IDIM], F32, kind="Internal").ap()

        stage_in = [sem(f"stage_in{s}") for s in range(RING)]
        w_hi, w_split, w_used = sem("w_hi"), sem("w_split"), sem("w_used")
        acc_evac = sem("acc_evac")
        silu_done, gh_ready = sem("silu_done"), sem("gh_ready")
        x_upd, sq_done, ssum_done = sem("x_upd"), sem("sq_done"), sem("ssum_done")
        xh_done, xl_done = sem("xh_done"), sem("xl_done")
        stat_done, var_done, sd_done, rstd_done = sem("stat_done"), sem("var_done"), sem("sd_done"), sem("rstd_done")
        const_in, x_in, ones_set, xt_done = sem("const_in"), sem("x_in"), sem("ones_set"), sem("xt_done")
        gain_ps, gain_set, g_ps, g_set, g_out = (sem("gain_ps"), sem("gain_set"), sem("g_ps"), sem("g_set"),
                                                 sem("g_out"))
        identb_in, kscr_in = sem("identb_in"), sem("kscr_in")
        fin_x, fin_ps, fin_sb = sem("fin_x"), sem("fin_ps"), sem("fin_sb")
        kiw_out, kv_out, y_out = sem("kiw_out"), sem("kv_out"), sem("y_out")
        carried = sem("carried")
        dve_step, act_step = sem("dve_step"), sem("act_step")
        MS = {L: {k: sem(k + L) for k in (
            "mix_in", "strip_in", "kiw_ps", "kiw_sb", "rep_ps", "wbl_set", "qis_set", "kist_in0", "kist_in1",
            "kict_ps", "kic_set", "dots_ps", "r_set", "r_usedS", "r_usedP", "s_evac", "kvt_ps", "kvt_sb",
            "vnew_ps", "vnew_sb", "qbd_set", "pmask_set", "maskS_set", "selb_in", "qk_ps", "nm_set", "p_set",
            "pt_ps", "pt_evac", "pv_ps", "es_in", "es_set", "o_evac", "ot_ps", "ot_evac", "kv_in", "kv_in0",
            "kv_in1", "kv_in2", "ktS_ps", "ktS_evac", "qkS_ps", "nmS_set", "psS_set", "ptS_ps", "ptS_evac",
            "ptnS_evac", "pvS_ps", "esS_in", "esS_set", "osS_set", "otS_ps", "otS_evac", "cm_used")} for L in "AB"}

        def used(n):
            return n + 1 + RING

        def over(name):
            n = dict(ffn=GU_CHUNKS + DN_CHUNKS, inA=A_CHUNKS, inB=B_CHUNKS, out=ND)
            return used(at[name][0] + n[name if name in n else name[:3]] - 1)

        def gh_base(name):
            return NF * int(name[3]) + 1

        norm_of = {0: 0, 1: 4, 2: 1, 3: 2, 4: 5, 5: 3}
        STAT = PS[3]

        def halves(ap):
            return ap.rearrange("p (h t) -> p h t", h=2)

        def gain(n, d):
            return gains[:, n * ND + d:n * ND + d + 1]

        def acc(k):
            return PS[k % RING][:, :, 0:HALF]

        block = ctx.enter_context(nc.Block())

        @block.sync
        def _(sp):
            def chunk(n, i, per, parts):
                s = n % RING
                sp.wait_ge(w_split, n + 1 + per * i)
                for dst, src in parts(WST[s]):
                    sp.dma_start(dst, src).then_inc(stage_in[s], 16)

            def cols(w, c0, width=P):
                v = w.rearrange("(b p) n -> p b n", p=P)

                def parts(st):
                    d = st[:, 0:ND * width].rearrange("p (b c) -> p b c", b=ND)
                    return [(d[h * 64:h * 64 + 64], v[h * 64:h * 64 + 64, :, bass.ds(c0, width)]) for h in range(2)]
                return parts

            def cols_of_group(w, g):
                v = w.rearrange("(b p) n -> p b n", p=P)

                def parts(st):
                    d = st[:, :].rearrange("p (b n c) -> p b n c", b=ND, n=KVH)
                    return [(d[:, :, n], v[:, :, (n * GRP + g) * HD:(n * GRP + g + 1) * HD]) for n in range(KVH)]
                return parts

            def ffn(name, l, s):
                n0 = at[name][0]
                wg, wu, wd = io["ffn_w_gate"][l, s], io["ffn_w_up"][l, s], io["ffn_w_down"][l, s]
                with sp.Fori(0, NF // RING) as i:
                    if name == "ffn0":
                        gather_keys(i)
                    for j in range(2 * RING):
                        chunk(n0 + j, i, 2 * RING, cols((wg, wu)[j % 2], (i * RING + j // 2) * P))
                if name == "ffn0":
                    for b in range(NF // RING, NB):
                        gather_keys(b)
                v = wd.rearrange("(q b p) n -> q p b n", q=RING, p=P)
                with sp.Fori(0, ND) as i:
                    for q in range(RING):
                        def parts(st):
                            d = st[:, 0:DB * P].rearrange("p (b c) -> p b c", b=DB)
                            return [(d[h * 64:h * 64 + 64], v[q, h * 64:h * 64 + 64, :, bass.ds(i * P, P)])
                                    for h in range(2)]
                        chunk(n0 + GU_CHUNKS + q, i, RING, parts)

            def project_out(name, w, first, last):
                n0 = at[name][0]
                v = w.rearrange("(n g d) m -> n d g m", n=KVH, d=HD)
                for t in range(first, last):
                    def parts(st):
                        d = st[:, :].rearrange("p (g c) -> p g c", g=GRP)
                        return [(d[n * HD:(n + 1) * HD], v[n, :, :, t * P:(t + 1) * P]) for n in range(KVH)]
                    chunk(n0 + t, 0, 0, parts)

            def pages_of(b):
                return nc.values_load_multi_w_load_instructions(
                    io["page_table"][b:b + 1, :] if isinstance(b, int) else io["page_table"][bass.ds(b, 1), :],
                    engines=[mybir.EngineType.SP], min_val=0, max_val=NPOOL - 1)[1]

            def gather_keys(b):
                for j, page in enumerate(pages_of(b)):
                    sp.dma_start(kscr[bass.ds(b * NPG + j, 1), :],
                                 io["cache_idx"][0, bass.ds(page, 1)].rearrange("a k d -> a (k d)"))\
                      .then_inc(kscr_in, 16)

            def kist(b):
                ms = MS["A"]
                if b == 0:
                    sp.wait_ge(kscr_in, 16 * NB * NPG)
                if b < 2:
                    sp.wait_ge(w_used, over("ffn0"))
                else:
                    sp.wait_ge(ms["kict_ps"], 2 * (b - 1))
                sp.dma_start(mixers["A"]["kist"][:, b % 2],
                             kscr[b * NPG:(b + 1) * NPG, :].rearrange("j (k d) -> k j d", d=IDIM))\
                  .then_inc(ms[f"kist_in{b % 2}"], 16)

            def kv_pages(b):
                ms = MS["A"]
                if b == 0:
                    sp.wait_ge(ms["pmask_set"], NQT - 1)
                elif b == 1:
                    sp.wait_ge(ms["ot_evac"], 2 * NQT)
                elif b == 2:
                    sp.wait_ge(ms["maskS_set"], 1)
                else:
                    sp.wait_ge(ms["pvS_ps"], b - KV_SLOTS + 1)
                for j, page in enumerate(pages_of(b)):
                    sp.dma_start(mixers["A"][f"kv{b % KV_SLOTS}"][:, j:j + 1, :],
                                 io["cache_kv"][0, bass.ds(page, 1)].rearrange("a k s n d -> k a (s n d)"))\
                      .then_inc(ms[f"kv_in{b % KV_SLOTS}"], 16)

            ffn("ffn0", 0, 0)
            w = io["a_w_in"][0]
            n0 = at["inA"][0]
            o_qi = QW + 2 * KVW
            todo = [cols(w, o_qi + IH * IDIM, IDIM + IH)] + [cols(w, o_qi + c * P) for c in range(IH // 2)]
            todo += [cols(w, QW), cols(w, QW + KVW)] + [cols_of_group(w, g) for g in range(GRP)]
            for c, parts in enumerate(todo):
                chunk(n0 + c, 0, 0, parts)
                if 2 <= c < 6:
                    kist(2 * (c - 2))
                    kist(2 * (c - 2) + 1)
            project_out("outA", io["a_w_out"][0], 0, RING)
            for b in range(NB):
                kv_pages(b)
            project_out("outA", io["a_w_out"][0], RING, ND)
            ffn("ffn1", 0, 1)
            ffn("ffn2", 1, 0)
            w = io["b_w_in"][0]
            todo = [cols(w, QW), cols(w, QW + KVW)] + [cols_of_group(w, g) for g in range(GRP)]
            for c, parts in enumerate(todo):
                chunk(at["inB"][0] + c, 0, 0, parts)
            project_out("outB", io["b_w_out"][0], 0, ND)
            ffn("ffn3", 1, 1)

        @block.gpsimd
        def _(pool):
            pool.memset(warm[:, 0:1], 0.0).then_inc(w_split, RING)
            pool.memset(warm[:, 1:2], 0.0).then_inc(w_used, RING)
            pool.memset(warm[:, 2:3], 0.0).then_inc(acc_evac, RING)
            pool.memset(warm[:, 3:4], 0.0).then_inc(gh_ready, 1)
            pool.dma_start(identb[:, :], io["c_ident"]).then_inc(identb_in, 16)

            def split(n, i, per, width):
                s = n % RING
                k = 0 if i is None else per * i
                pool.wait_ge(stage_in[s], 32 * (n // RING + 1) + (0 if i is None else 32 * (per // RING) * i))
                pool.wait_ge(w_used, n + 1 + k)
                if i is not None:
                    pool.sem_inc(carried, 1)
                nc.gpsimd.tensor_copy(WSP[s][:, 0, 0:width], WST[s][:, 0:width]).then_inc(w_hi, 1)
                pool.wait_ge(w_hi, n + 1 + k)
                nc.gpsimd.tensor_tensor(WSP[s][:, 1, 0:width], WST[s][:, 0:width],
                                        WSP[s][:, 0, 0:width].bitcast(F32), ALU.subtract).then_inc(w_split, 1)

            def ffn(name):
                n0 = at[name][0]
                with pool.Fori(0, NF // RING) as i:
                    for j in range(2 * RING):
                        split(n0 + j, i, 2 * RING, ND * P)
                with pool.Fori(0, ND) as i:
                    for q in range(RING):
                        split(n0 + GU_CHUNKS + q, i, RING, DB * P)

            ffn("ffn0")
            pool.wait_ge(w_used, over("ffn0"))
            pool.dma_start(mixers["A"]["selb"][:, :, :], io["c_selb"].rearrange("s (b r) -> s b r", b=NB))\
                .then_inc(MS["A"]["selb_in"], 16)
            for c in range(A_CHUNKS):
                split(at["inA"][0] + c, None, 0, ND * (IDIM + IH) if c == 0 else ND * P)
            for t in range(ND):
                split(at["outA"][0] + t, None, 0, ND * P)
            ffn("ffn1")
            ffn("ffn2")
            for c in range(B_CHUNKS):
                split(at["inB"][0] + c, None, 0, ND * P)
            for t in range(ND):
                split(at["outB"][0] + t, None, 0, ND * P)
            ffn("ffn3")

        @block.tensor
        def _(pe):
            mm = nc.tensor.matmul

            def mm3(out, slot, b, width, H, L, first, last):
                w = WSP[slot]
                for k, (part, x) in enumerate(((0, H), (0, L), (1, H))):
                    for h in range(2):
                        ins = mm(out[0:width, h, :], w[:, part, b * width:(b + 1) * width],
                                 x[:, h * HALF:(h + 1) * HALF], start=first and k == 0, stop=last and k == 2)
                return ins

            def statistics(e):
                pe.wait_ge(ssum_done, 8 * e + 8)
                for h in range(2):
                    ins = mm(STAT[:, h, 0:HALF], ones[:, :], ssum[:, h * HALF:(h + 1) * HALF], start=True, stop=True)
                ins.then_inc(stat_done, 1)

            def project(n, a, i, per, width):
                k = 0 if i is None else per * i
                pe.wait_ge(w_split, n + 1 + RING + k)
                pe.wait_ge(acc_evac, a + 1 + k)
                for b in range(ND):
                    ins = mm3(acc(a), n % RING, b, width, XH[:, b, :], XL[:, b, :], b == 0, b == ND - 1)
                ins.then_inc(w_used, 1)

            def ffn(name):
                n0, a0, e = at[name]
                pe.wait_ge(xl_done, 8 * e)
                statistics(e - 1)
                with pe.Fori(0, NF // RING) as i:
                    for j in range(2 * RING):
                        project(n0 + j, a0 + j, i, 2 * RING, P)
                aend = a0 + GU_CHUNKS
                pe.wait_ge(acc_evac, aend - 1 + RING)
                with pe.Fori(0, ND // 2) as i:
                    for j in range(2):
                        pe.wait_ge(x_upd, 8 * e + j - 1 + 2 * i)
                        for q in range(RING):
                            n = n0 + GU_CHUNKS + j * RING + q
                            pe.wait_ge(w_split, n + 1 + RING + 2 * RING * i)
                            pe.wait_ge(gh_ready, gh_base(name) + DB * (q + 1))
                            for b in range(DB):
                                ins = mm3(acc(aend + j), n % RING, b, P, GH[:, q * DB + b, :], GL[:, q * DB + b, :],
                                          q == 0 and b == 0, q == RING - 1 and b == DB - 1)
                            ins.then_inc(w_used, 1)

            def project_out(name, aend):
                n0, _, e = at[name]
                for t in range(ND):
                    n = n0 + t
                    if t > 1:
                        pe.wait_ge(x_upd, 8 * e + t - 1)
                    pe.wait_ge(w_split, n + 1 + RING)
                    for b in range(ND):
                        ins = mm3(acc(aend + t % 2), n % RING, b, P, XH[:, b, :], XL[:, b, :], b == 0, b == ND - 1)
                    ins.then_inc(w_used, 1)

            def mixer_new_rows(m, ms, a, first_bank):
                pe.wait_ge(acc_evac, a + RING)
                for t in range(NTT):
                    w = min(P, TOK - t * P)
                    if t > 1:
                        pe.wait_ge(ms["kvt_sb"], t - 1)
                    bk = bank[6 + t % 2]
                    nc.tensor.transpose(bk[0:w, 0:P], m["kT"][:, t * P:t * P + w], ident[:, :])
                    nc.tensor.transpose(bk[0:w, P:2 * P], m["vT"][:, t * P:t * P + w], ident[:, :])\
                        .then_inc(ms["kvt_ps"], 1)
                for h in range(2):
                    pe.wait_ge(ms["kvt_sb"], NTT - 1 + h)
                    bk = bank[6 + (NTT + h) % 2]
                    for k in range(NB // 2):
                        b = h * NB // 2 + k
                        ins = nc.tensor.transpose(bk[0:NT, k * P:(k + 1) * P],
                                                  m["vT"][:, SEQ + b * NT:SEQ + (b + 1) * NT], ident[:, :])
                    ins.then_inc(ms["vnew_ps"], 1)

            def prompt_attention(L, m, ms, aend):
                units = [(i, g) for i in range(NQT) for g in range(GRP)]
                pe.wait_ge(acc_evac, aend + RING)
                pe.wait_ge(ms["kvt_sb"], NTT)
                pe.wait_ge(ms["vnew_sb"], 2)

                def logits(u):
                    i, g = units[u]
                    k0, nk = key_range(L, i)
                    if u > 1:
                        pe.wait_ge(ms["p_set"], 2 * (u - 1))
                    masked = L == "A" and i > 0
                    if masked:
                        pe.wait_ge(ms["pmask_set"], i)
                        pe.wait_ge(identb_in, 16)
                        for n in range(KVH):
                            mm(PS[u % 2][:, n, 0:nk], identb[:, :], m["pmask"][:, i - 1, 0:nk], start=True, stop=False)
                    for n in range(KVH):
                        h = slice(n * HD, (n + 1) * HD)
                        ins = mm(PS[u % 2][:, n, 0:nk], m["qT"][h, g, i * P:(i + 1) * P], m["kT"][h, k0:k0 + nk],
                                 start=not masked, stop=True)
                    ins.then_inc(ms["qk_ps"], 1)

                logits(0)
                logits(1)
                for u, (i, g) in enumerate(units):
                    k0, nk = key_range(L, i)
                    if g == 0 and i > 0:
                        pe.wait_ge(ms["ot_evac"], 2 * i)
                    for n in range(KVH):
                        pe.wait_ge(ms["p_set"], 2 * u + n + 1)
                        if u > 0:
                            pe.wait_ge(ms["pt_evac"], 2 * u - 1 + n)
                        for k in range(nk // P):
                            ins = nc.tensor.transpose(bank[4 + n][:, k * P:(k + 1) * P],
                                                      m["p"][:, u % 2, n, k * P:(k + 1) * P], ident[:, :])
                        ins.then_inc(ms["pt_ps"], 1)
                    if u + 2 < len(units):
                        logits(u + 2)
                    for n in range(KVH):
                        pe.wait_ge(ms["pt_evac"], 2 * u + n + 1)
                        if g == 0 and i > 0:
                            pe.wait_ge(ms["o_evac"], 2 * i)
                        for k in range(nk // P):
                            ins = mm(bank[6 + n][:, g * HD:(g + 1) * HD], m["pt"][:, n, k, :],
                                     m["kvtok"][:, k0 // P + k, KVW + n * HD:KVW + (n + 1) * HD],
                                     start=k == 0, stop=k == nk // P - 1)
                        ins.then_inc(ms["pv_ps"], 1)
                    if g == GRP - 1:
                        pe.wait_ge(ms["o_evac"], 2 * i + 2)
                        for h in range(2):
                            pe.wait_ge(ms["pt_evac"], 2 * u + 2)
                            for k in range(4):
                                ins = nc.tensor.transpose(bank[4 + h][:, k * P:(k + 1) * P],
                                                          m["otok"][:, 4 * h + k, :, :], ident[:, :])
                            ins.then_inc(ms["ot_ps"], 1)

            def paged_sample_attention(m, ms):
                ktg, ptg, ring = KT_TILES, PT_TILES, sample_order()
                LG = sample_logits
                pe.wait_ge(ms["ot_evac"], 2 * NQT)
                pe.wait_ge(ms["qbd_set"], 1)
                pe.wait_ge(ms["maskS_set"], 1)
                pe.wait_ge(ms["selb_in"], 16)

                def bank_of(kind, b, k):
                    at_ = ring.index((kind, b, k))
                    if at_ > 1:
                        kind0, b0, k0 = ring[at_ - 2]
                        if kind0 == "kt":
                            pe.wait_ge(ms["ktS_evac"], b0 * len(ktg) + k0 + 1)
                        else:
                            pe.wait_ge(ms["ptS_evac"], b0 * len(ptg) + k0 + 1)
                    return bank[5 + at_ % 2]

                def keys(b):
                    pe.wait_ge(ms[f"kv_in{b % KV_SLOTS}"], 16 * NPG * (b // KV_SLOTS + 1))
                    for k, pages in enumerate(ktg):
                        bk = bank_of("kt", b, k)
                        for c, j in enumerate(pages):
                            ins = nc.tensor.transpose(bk[:, c * P:(c + 1) * P], m[f"kv{b % KV_SLOTS}"][:, j, 0:KVW],
                                                      ident[:, :])
                        ins.then_inc(ms["ktS_ps"], 1)

                def logits(b):
                    pe.wait_ge(ms["ktS_evac"], len(ktg) * (b + 1))
                    if b:
                        pe.wait_ge(ms["psS_set"], b)
                    q = m["qbd"][:, b, :]
                    for c in range(0, NPG * PAGE, SEQ):
                        w = min(SEQ, NPG * PAGE - c)
                        mm(LG[:, c:c + w], m["selb"][:, b, :], m["maskS"][:, c:c + w], start=True, stop=False)
                        mm(LG[:, c:c + w], q, m["KT"][:, b % 2, c:c + w], start=False, stop=True)
                    c = NPG * PAGE
                    mm(LG[:, c:c + NT], m["selb"][:, b, :], m["maskS"][:, c:c + NT], start=True, stop=False)
                    mm(LG[:, c:c + NT], q, m["kT"][:, SEQ + b * NT:SEQ + (b + 1) * NT], start=False, stop=True)\
                        .then_inc(ms["qkS_ps"], 1)

                def weights_transposed(b):
                    pe.wait_ge(ms["psS_set"], b + 1)
                    for k, tiles in enumerate(ptg):
                        bk = bank_of("pt", b, k)
                        for c, j in enumerate(tiles):
                            w = P if j < NPG else NT
                            ins = nc.tensor.transpose(bk[0:w, c * P:(c + 1) * P], m["ps"][:, j * P:j * P + w],
                                                      ident[:, :])
                        ins.then_inc(ms["ptS_ps"], 1)

                def values(b):
                    pe.wait_ge(ms["ptS_evac"], len(ptg) * (b + 1))
                    if b:
                        pe.wait_ge(ms["otS_evac"], b)
                    for j in range(NPG):
                        mm(bank[7][:, 0:P], m["pts"][:, j, :], m[f"kv{b % KV_SLOTS}"][:, j, KVW:2 * KVW], start=j == 0,
                           stop=False)
                    mm(bank[7][:, 0:P], m["pts"][0:NT, NPG, :], m["vnew"][:, b, :], start=False, stop=True)\
                        .then_inc(ms["pvS_ps"], 1)

                def outputs_transposed(b):
                    pe.wait_ge(ms["osS_set"], b + 1)
                    nc.tensor.transpose(bank[7][:, P:2 * P], m["os"][:, :], ident[:, :]).then_inc(ms["otS_ps"], 1)

                keys(0)
                logits(0)
                keys(1)
                for b in range(NB):
                    if b + 1 < NB:
                        logits(b + 1)
                    if b:
                        outputs_transposed(b - 1)
                    weights_transposed(b)
                    if b + 2 < NB:
                        keys(b + 2)
                    values(b)
                outputs_transposed(NB - 1)
                pe.wait_ge(ms["otS_evac"], NB)

            def window_sample_attention(m, ms):
                pe.wait_ge(ms["ot_evac"], 2 * NQT)
                pe.wait_ge(ms["qbd_set"], 1)
                pe.wait_ge(ms["kv_in"], 16)
                for b in range(NB):
                    ins = nc.tensor.transpose(bank[3 + b // HALF_B][:, b % HALF_B * P:(b % HALF_B + 1) * P],
                                              m["kv"][:, b, 0:KVW], ident[:, :])
                    if b % HALF_B == HALF_B - 1:
                        ins.then_inc(ms["ktS_ps"], 1)
                for k, group in enumerate(LOGIT_GROUPS):
                    pe.wait_ge(ms["ktS_evac"], group[-1] // HALF_B + 1)
                    for c, b in enumerate(group):
                        q, c0 = m["qbd"][:, b, :], c * NEAR
                        mm(bank[k][:, c0:c0 + P], q, m["KT"][:, b, :], start=True, stop=True)
                        ins = mm(bank[k][:, c0 + P:c0 + NEAR], q, m["kT"][:, SEQ + b * NT:SEQ + (b + 1) * NT],
                                 start=True, stop=True)
                    ins.then_inc(ms["qkS_ps"], 1)
                for half in range(2):
                    for c in range(HALF_B):
                        b = half * HALF_B + c
                        pe.wait_ge(ms["psS_set"], b + 1)
                        at_ = slice(c * P, (c + 1) * P)
                        nc.tensor.transpose(bank[5 + half][:, at_], m["ps"][:, b, 0:P], ident[:, :])
                        ins = nc.tensor.transpose(bank[(7, 3)[half]][0:NT, at_], m["ps"][:, b, P:NEAR], ident[:, :])
                    ins.then_inc(ms["ptS_ps"], 1)
                for half in range(2):
                    pe.wait_ge(ms["ptS_evac"], half + 1)
                    pe.wait_ge(ms["ptnS_evac"], half + 1)
                    for c in range(HALF_B):
                        b = half * HALF_B + c
                        out = bank[(4, 0)[half]][:, c * P:(c + 1) * P]
                        mm(out, m["pts"][:, b, :], m["kv"][:, b, KVW:2 * KVW], start=True, stop=False)
                        ins = mm(out, m["ptsn"][:, b, :], m["vnew"][:, b, :], start=False, stop=True)
                    ins.then_inc(ms["pvS_ps"], 1)
                for half in range(2):
                    pe.wait_ge(ms["osS_set"], half + 1)
                    for c in range(HALF_B):
                        ins = nc.tensor.transpose(bank[1 + half][:, c * P:(c + 1) * P],
                                                  m["os"][:, half * HALF_B + c, :], ident[:, :])
                    ins.then_inc(ms["otS_ps"], 1)
                pe.wait_ge(ms["otS_evac"], 2)

            def indexer(m, ms, a0):
                u = 0
                pe.wait_ge(ms["qis_set"], 1)
                pe.wait_ge(ms["wbl_set"], 1)
                pe.wait_ge(ms["kic_set"], 2 * NB)
                pe.wait_ge(acc_evac, a0 + 3 + RING)
                groups = [(e, q) for q in range(2) for e in range(2)] + [None]
                todo = [(k, gr, j) for k, gr in enumerate(groups) for j in range(NB // 2)]

                def dots(u, k, gr, j):
                    if u > 1:
                        pe.wait_ge(ms["r_set"], u - 1)
                    else:
                        pe.wait_ge(ms["kic_set"], 2 * NB)
                    for bb in range(2):
                        b = 2 * j + bb
                        e = gr[0] if gr else 0
                        h = slice(e * IDIM, (e + 1) * IDIM)
                        w = SEQ if gr else NT
                        keys = m["kic"][h, b, 4 * gr[1]:4 * gr[1] + 4, :] if gr else \
                            m["kiT"][h, SEQ + b * NT:SEQ + (b + 1) * NT]
                        ins = mm(bank[6 + u % 2][bb * 64:(bb + 1) * 64, 0:w], m["qiS"][h, b, :, :], keys,
                                 start=True, stop=True)
                    ins.then_inc(ms["dots_ps"], 1)

                def weigh(u, k, gr, j):
                    w = SEQ if gr else NT
                    pe.wait_ge(ms["r_set"], u + 1)
                    if j == 0 and k > 1:
                        pe.wait_ge(ms["s_evac"], k - 1)
                    ins = mm(bank[4 + k % 2][0:NS, 0:w], m["wbl"][:, j, :], m["r"][:, u % 2, 0:w],
                             start=j == 0, stop=j == NB // 2 - 1)
                    ins.then_inc(ms["r_usedS"], 1)

                for u, (k, gr, j) in enumerate(todo):
                    dots(u, k, gr, j)
                    if u:
                        weigh(u - 1, *todo[u - 1])
                weigh(u, *todo[u])
                u = len(todo)
                for i in range(1, NQT):
                    for h in range(IH):
                        pe.wait_ge(ms["r_set"], u - 1)
                        s = slice(h % 2 * IDIM, (h % 2 + 1) * IDIM)
                        mm(bank[6 + u % 2][:, 0:(i + 1) * P], m["qiT"][s, h // 2, i * P:(i + 1) * P],
                           m["kiT"][s, 0:(i + 1) * P], start=True, stop=True).then_inc(ms["dots_ps"], 1)
                        u += 1
                pe.wait_ge(ms["r_set"], u)

            pe.wait_ge(const_in, 16 * N_CONST)
            pe.wait_ge(ones_set, 1)
            nc.tensor.transpose(bank[6][:, 0:7 * ND], grows[:, :], ident[0:7 * ND, 0:7 * ND]).then_inc(gain_ps, 1)
            mm(bank[7][0:HEADS, 0:GW], tabx[:, :], coef[:, :], start=True, stop=True).then_inc(g_ps, 1)
            pe.wait_ge(x_in, 16 * NTT)
            for d in range(ND):
                if d > 2:
                    pe.wait_ge(x_upd, d - 2)
                for t in range(NTT):
                    w = min(P, TOK - t * P)
                    ins = nc.tensor.transpose(PS[d % RING][:, t // 4, t % 4 * P:t % 4 * P + w],
                                              xtok[0:w, t, d * P:(d + 1) * P], ident[0:w, 0:w])
                ins.then_inc(xt_done, 1)

            ffn("ffn0")
            m, ms = mixers["A"], MS["A"]
            n0, a0, e = at["inA"]
            pe.wait_ge(xl_done, 8 * e)
            statistics(e - 1)
            pe.wait_ge(rstd_done, e)
            for c in range(1 + IH // 2):
                project(n0 + c, a0 + c, None, 0, IDIM + IH if c == 0 else P)
                if c:
                    for b in (2 * c - 2, 2 * c - 1):
                        pe.wait_ge(ms[f"kist_in{b % 2}"], 16 * (b // 2 + 1))
                        for h in range(2):
                            if b:
                                pe.wait_ge(ms["kic_set"], 2 * b - 1 + h)
                            for k in range(4):
                                ins = nc.tensor.transpose(
                                    bank[6 + h][:, k * P:(k + 1) * P],
                                    m["kist"][:, b % 2, 8 * h + 2 * k:8 * h + 2 * k + 2, :], ident[:, :])
                            ins.then_inc(ms["kict_ps"], 1)
            pe.wait_ge(ms["kic_set"], 2 * NB)
            for t in range(NTT):
                w = min(P, TOK - t * P)
                nc.tensor.transpose(bank[6][0:w, t * 72:t * 72 + IDIM], m["kiT"][0:IDIM, t * P:t * P + w],
                                    ident[0:IDIM, 0:IDIM])
                ins = nc.tensor.transpose(bank[6][0:w, t * 72 + IDIM:(t + 1) * 72],
                                          sq[IDIM:IDIM + IH, t * P:t * P + w], ident[IDIM:IDIM + IH, IDIM:IDIM + IH])
            ins.then_inc(ms["kiw_ps"], 1)
            pe.wait_ge(ms["mix_in"], 16 * N_MIX["A"])
            mm(bank[7][:, 0:NS], m["rep"][IDIM:IDIM + IH, :], sq[IDIM:IDIM + IH, SEQ:TOK], start=True, stop=True)\
                .then_inc(ms["rep_ps"], 1)
            pe.wait_ge(ms["kiw_sb"], 1)
            indexer(m, ms, a0)
            c = 1 + IH // 2
            pe.wait_ge(ms["s_evac"], 5)
            for c in range(c, c + 3):
                project(n0 + c, a0 + c, None, 0, P)
            mixer_new_rows(m, ms, a0 + c, 6)
            for c in range(c + 1, A_CHUNKS):
                project(n0 + c, a0 + c, None, 0, P)
            aend = a0 + A_CHUNKS
            prompt_attention("A", m, ms, aend)
            paged_sample_attention(m, ms)
            project_out("outA", aend)
            ffn("ffn1")
            ffn("ffn2")
            m, ms = mixers["B"], MS["B"]
            n0, a0, e = at["inB"]
            pe.wait_ge(xl_done, 8 * e)
            statistics(e - 1)
            pe.wait_ge(rstd_done, e)
            for c in range(3):
                project(n0 + c, a0 + c, None, 0, P)
            mixer_new_rows(m, ms, a0 + c, 6)
            for c in range(c + 1, B_CHUNKS):
                project(n0 + c, a0 + c, None, 0, P)
            aend = a0 + B_CHUNKS
            prompt_attention("B", m, ms, aend)
            window_sample_attention(m, ms)
            project_out("outB", aend)
            ffn("ffn3")
            pe.wait_ge(x_upd, 8 * 7)
            statistics(6)
            for t in range(NTT):
                w = min(P, TOK - t * P)
                for h in range(2):
                    k = 2 * t + h
                    pe.wait_ge(fin_x, 4 * h + 4)
                    if k > 2:
                        pe.wait_ge(fin_sb, k - 2)
                    for c in range(4):
                        ins = nc.tensor.transpose(PS[k % 3][0:w, 0, c * P:(c + 1) * P], X[:, 4 * h + c, t * P:t * P + w],
                                                  ident[:, :])
                    ins.then_inc(fin_ps, 1)

        @block.scalar
        def _(act):
            fn = nc.scalar.activation
            steps = Steps(act, act_step)

            def update(e, deferred=False):
                def high(d):
                    fn(XH[:, d, :], X[:, d, :], ACT.Copy, scale=gain(norm_of[e], d)).then_inc(xh_done, 1)
                for d in range(ND):
                    act.wait_ge(x_upd, 8 * e + d + 1)
                    if e or d:
                        act.wait_ge(ssum_done, 8 * e + d)
                    fn(sq[:, :], X[:, d, :], ACT.Square).then_inc(sq_done, 1)
                    if e in norm_of and not deferred:
                        high(d)
                if deferred:
                    act.wait_ge(w_used, over({2: "outA", 5: "outB"}[e]))
                    for d in range(ND):
                        high(d)

            def root(e):
                act.wait_ge(var_done, e + 1)
                fn(rstd[:, :], rstd[:, :], ACT.Sqrt).then_inc(sd_done, 1)

            def ffn(name):
                n0, a0, e = at[name]
                root(e - 1)
                with act.Fori(0, NF // RING) as i:
                    for j in range(RING):
                        act.wait_ge(acc_evac, RING + a0 + 2 * j + 1 + 2 * RING * i)
                        fn(gs[:, j % 2, :], gs[:, j % 2, :], ACT.Silu).then_inc(silu_done, 1)

            def copy_rows(m, ms, L):
                for t in range(NTT):
                    w = min(P, TOK - t * P)
                    act.wait_ge(ms["kvt_ps"], t + 1)
                    fn(m["kvtok"][0:w, t, :], bank[6 + t % 2][0:w, 0:2 * KVW], ACT.Copy).then_inc(ms["kvt_sb"], 1)
                for h in range(2):
                    act.wait_ge(ms["vnew_ps"], h + 1)
                    fn(m["vnew"][:, 4 * h:4 * h + 4, :],
                       bank[6 + (NTT + h) % 2][0:NT, :].rearrange("t (b c) -> t b c", b=4), ACT.Copy)\
                        .then_inc(ms["vnew_sb"], 1)
                act.wait_ge(ms["kvt_sb"], NTT)

            def attention_loads(m, ms):
                act.wait_ge(g_out, 16)
                act.dma_start(m["strip"].rearrange("p n g x -> p (n g) x"),
                              bass.AP(tensor=gscr, offset=P - 1, ap=[[SKEW, P], [GW, HEADS], [1, 2 * P]]))\
                    .then_inc(ms["strip_in"], 16)
                for h in range(HEADS):
                    act.dma_start(m["biasS"][h * NT:(h + 1) * NT, :],
                                  bass.AP(tensor=gscr, offset=h * GW + P - 1, ap=[[SKEW, NT], [1, NEAR]]))\
                        .then_inc(ms["strip_in"], 16)

            def prompt_attention(L, m, ms):
                units = [(i, g) for i in range(NQT) for g in range(GRP)]

                def exps(u):
                    i, g = units[u]
                    nk = key_range(L, i)[1]
                    act.wait_ge(ms["nm_set"], u + 1)
                    if u > 1:
                        act.wait_ge(ms["pt_ps"], 2 * (u - 1))
                    for n in range(KVH):
                        fn(m["p"][:, u % 2, n, 0:nk], PS[u % 2][:, n, 0:nk], ACT.Exp,
                           bias=m["nm"][:, i, n, g:g + 1], accum_out=m["rs"][:, i, n, g:g + 1])\
                            .then_inc(ms["p_set"], 1)

                exps(0)
                for u, (i, g) in enumerate(units):
                    if u + 1 < len(units):
                        exps(u + 1)
                    nk = key_range(L, i)[1]
                    for n in range(KVH):
                        act.wait_ge(ms["pt_ps"], 2 * u + n + 1)
                        if u:
                            act.wait_ge(ms["pv_ps"], 2 * u - 1 + n)
                        fn(m["pt"][:, n, 0:nk // P, :].rearrange("p a b -> p (a b)"), bank[4 + n][:, 0:nk], ACT.Copy)\
                            .then_inc(ms["pt_evac"], 1)
                    if L == "B" and g == GRP - 1:
                        act.wait_ge(ms["es_in"], i + 1)
                        fn(m["es"][:, :, :], m["es"][:, :, :], ACT.Exp).then_inc(ms["es_set"], 1)

            def paged_sample_attention(m, ms):
                ring = sample_order()

                def keys(b):
                    for k, pages in enumerate(KT_TILES):
                        act.wait_ge(ms["ktS_ps"], b * KT_GROUPS + k + 1)
                        if b > 1:
                            act.wait_ge(ms["qkS_ps"], b - 1)
                        w = len(pages) * P
                        fn(m["KT"][:, b % 2, pages[0] * P:pages[0] * P + w],
                           bank[5 + ring.index(("kt", b, k)) % 2][:, 0:w], ACT.Copy).then_inc(ms["ktS_evac"], 1)

                def exps(b):
                    act.wait_ge(ms["nmS_set"], b + 1)
                    if b:
                        act.wait_ge(ms["ptS_ps"], PT_GROUPS * b)
                    fn(m["ps"][:, :], sample_logits[:, 0:KEYS], ACT.Exp,
                       bias=m["nmS"][:, b:b + 1], accum_out=m["rsS"][:, b:b + 1]).then_inc(ms["psS_set"], 1)

                keys(0)
                keys(1)
                exps(0)
                for b in range(NB):
                    if b + 1 < NB:
                        exps(b + 1)
                    if b + 2 < NB:
                        keys(b + 2)

            def window_sample_attention(m, ms):
                for half in range(2):
                    act.wait_ge(ms["ktS_ps"], half + 1)
                    fn(m["KT"][:, half * HALF_B:(half + 1) * HALF_B, :].rearrange("p b k -> p (b k)"),
                       bank[3 + half][:, :], ACT.Copy).then_inc(ms["ktS_evac"], 1)
                for k, group in enumerate(LOGIT_GROUPS):
                    act.wait_ge(ms["nmS_set"], k + 1)
                    for c, b in enumerate(group):
                        fn(m["ps"][:, b, :], bank[k][:, c * NEAR:(c + 1) * NEAR], ACT.Exp,
                           bias=m["nmS"][:, b:b + 1], accum_out=m["rsS"][:, b:b + 1]).then_inc(ms["psS_set"], 1)
                act.wait_ge(ms["esS_in"], 1)
                fn(m["esS"][:, :], m["esS"][:, :], ACT.Exp).then_inc(ms["esS_set"], 1)
                for half in range(2):
                    act.wait_ge(ms["ptS_ps"], half + 1)
                    fn(m["ptsn"][:, half * HALF_B:(half + 1) * HALF_B, :].rearrange("p b k -> p (b k)"),
                       bank[(7, 3)[half]][0:NT, :], ACT.Copy).then_inc(ms["ptnS_evac"], 1)

            for dst, src in ((ident[:, :], io["c_ident"]), (grows[0:4 * ND, :], io["ffn_norm"].rearrange(
                    "l s (d p) -> (l s d) p", p=P)), (grows[4 * ND:6 * ND, :], io["mix_norm"].rearrange(
                    "l (d p) -> (l d) p", p=P)), (grows[6 * ND:7 * ND, :], io["final_norm"].rearrange(
                    "(d p) -> d p", p=P)), (tabx[0:NBUCK, :], io["rel_bias"]), (coef[:, :], io["c_coef"])):
                act.dma_start(dst, src).then_inc(const_in, 16)
            for t in range(NTT):
                src = io["x_prompt"][0, t * P:(t + 1) * P, :] if t < NQT else \
                    io["x_sample"].rearrange("b t d -> (b t) d")
                act.dma_start(xtok[0:src.shape[0], t, :], src).then_inc(x_in, 16)
            act.wait_ge(gain_ps, 1)
            fn(gains[:, :], bank[6][:, 0:7 * ND], ACT.Copy).then_inc(gain_set, 1)
            act.wait_ge(g_ps, 1)
            fn(gvec[:, :], bank[7][0:HEADS, 0:GW], ACT.Copy).then_inc(g_set, 1)
            act.wait_ge(g_set, 1)
            act.dma_start(bass.AP(tensor=gscr, offset=0, ap=[[GW, HEADS], [SKEW + 1, P], [1, GW]]),
                          gvec[:, :].unsqueeze(1).to_broadcast([HEADS, P, GW])).then_inc(g_out, 16)
            act.wait_ge(gain_set, 1)
            update(0)
            act.wait_ge(g_out, 16)
            ffn("ffn0")
            update(1)
            m, ms = mixers["A"], MS["A"]
            act.wait_ge(w_used, over("ffn0"))
            act.wait_ge(gh_ready, gh_base("ffn1"))
            for name, key in (("pairm", "c_pairm"), ("cmask", "c_cmask"), ("rep", "c_rep"), ("tailm", "c_tailm")):
                dst = m[name]
                dst = dst.rearrange("p a b -> p (a b)") if name == "pairm" else dst[:, :]
                act.dma_start(dst, io[key]).then_inc(ms["mix_in"], 16)
            root(1)
            for b in range(NB):
                for h in range(2):
                    act.wait_ge(ms["kict_ps"], 2 * b + h + 1)
                    fn(m["kic"][:, b, 4 * h:4 * h + 4, :].rearrange("p a b -> p (a b)"), bank[6 + h][:, :], ACT.Copy)\
                        .then_inc(ms["kic_set"], 1)
            act.wait_ge(ms["kiw_ps"], 1)
            kw = IDIM + IH
            fn(m["kiw"][:, 0:NQT, :].rearrange("p a b -> p (a b)"), bank[6][:, 0:NQT * kw], ACT.Copy)
            fn(m["kiw"][0:NS, NQT, :], bank[6][0:NS, NQT * kw:NTT * kw], ACT.Copy).then_inc(ms["kiw_sb"], 1)
            act.wait_ge(ms["kiw_sb"], 1)
            act.dma_start(io["new_idx_prompt"][0, 0].rearrange("(t p) d -> p t d", p=P),
                          m["kiw"][:, 0:NQT, 0:IDIM]).then_inc(kiw_out, 16)
            act.dma_start(io["new_idx_sample"][0].rearrange("b t d -> (b t) d"), m["kiw"][0:NS, NQT, 0:IDIM])\
                .then_inc(kiw_out, 16)
            nS = 5 * NB // 2
            for u in range(nS + (NQT - 1) * IH):
                act.wait_ge(ms["dots_ps"], u + 1)
                if 1 < u < nS + 2:
                    act.wait_ge(ms["r_usedS"], u - 1)
                elif u >= nS + 2:
                    act.wait_ge(ms["r_usedP"], u - nS - 1)
                w = (NT if u >= nS - NB // 2 else SEQ) if u < nS else ((u - nS) // IH + 2) * P
                fn(m["r"][:, u % 2, 0:w], bank[6 + u % 2][:, 0:w], ACT.Relu, scale=IDIM ** -0.5)\
                    .then_inc(ms["r_set"], 1)
            copy_rows(m, ms, "A")
            act.dma_start(io["new_kv_prompt"][0, 0].rearrange("(t p) s n d -> p t (s n d)", p=P),
                          m["kvtok"][:, 0:NQT, :]).then_inc(kv_out, 16)
            act.dma_start(io["new_kv_sample"][0].rearrange("b t s n d -> (b t) (s n d)"), m["kvtok"][0:NS, NQT, :])\
                .then_inc(kv_out, 16)
            act.wait_ge(ms["r_usedP"], (NQT - 1) * IH)
            act.wait_ge(ms["cm_used"], NQT - 1)
            act.wait_ge(kiw_out, 32)
            attention_loads(m, ms)
            prompt_attention("A", m, ms)
            paged_sample_attention(m, ms)
            act.wait_ge(kv_out, 32)
            update(2, deferred=True)
            ffn("ffn1")
            update(3)
            ffn("ffn2")
            update(4)
            m, ms = mixers["B"], MS["B"]
            act.wait_ge(w_used, over("ffn2"))
            act.wait_ge(gh_ready, gh_base("ffn3"))
            act.dma_start(m["kv"][:, :, :], io["state_win_kv"][0].rearrange("b k s n d -> k b (s n d)"))\
                .then_inc(ms["kv_in"], 16)
            act.dma_start(io["new_win_sample"][0, :, 0:P - NT].rearrange("b k s n d -> b (k s n d)"),
                          io["state_win_kv"][0, :, NT:P].rearrange("b k s n d -> b (k s n d)")).then_inc(kv_out, 16)
            sinks, last = io["b_sinks"][0], io["rel_bias"][NBUCK - 1]
            for dst, src in ((m["wm"][:, :], io["c_wmask"]), (m["wmS"][:, :], io["c_wmaskS"])):
                act.dma_start(dst, src).then_inc(ms["mix_in"], 16)
            with nc.allow_non_contiguous_dma(reason="16 numbers, spread over the rows of the heads"):
                for row, wide, tall in ((sinks, m["nsink"], m["nsinkS"][:, :]), (last, m["es"], m["esS"][:, 0:1])):
                    act.dma_start(wide.rearrange("p n g -> p (n g)"),
                                  bass.AP(tensor=row.tensor, offset=row.offset, ap=[[0, P], [1, HEADS]]))\
                        .then_inc(ms["mix_in"], 16)
                    act.dma_start(tall, bass.AP(tensor=row.tensor, offset=row.offset,
                                                ap=[[1, HEADS], [0, NT], [1, 1]])).then_inc(ms["mix_in"], 16)
            root(4)
            copy_rows(m, ms, "B")
            attention_loads(m, ms)
            act.dma_start(io["new_win_prompt"][0, 0].rearrange("k s n d -> k (s n d)"), m["kvtok"][:, NQT - 1, :])\
                .then_inc(kv_out, 16)
            act.dma_start(io["new_win_sample"][0, :, P - NT:P].rearrange("b k s n d -> b k (s n d)"),
                          m["kvtok"][0:NS, NQT, :]).then_inc(kv_out, 16)
            prompt_attention("B", m, ms)
            window_sample_attention(m, ms)
            act.wait_ge(kv_out, 16 * 5)
            update(5, deferred=True)
            ffn("ffn3")
            update(6)
            root(6)
            for t in range(NTT):
                w = min(P, TOK - t * P)
                for h in range(2):
                    k = 2 * t + h
                    act.wait_ge(fin_ps, k + 1)
                    fn(xtok[0:w, t, h * SEQ:(h + 1) * SEQ], PS[k % 3][0:w, 0, :], ACT.Copy).then_inc(fin_sb, 1)
                act.wait_ge(fin_sb, 2 * t + 2)
                dst = io["y_prompt"][0, t * P:(t + 1) * P, :] if t < NQT else \
                    io["y_sample"].rearrange("b t d -> (b t) d")
                act.dma_start(dst, xtok[0:w, t, :]).then_inc(y_out, 16)
            act.wait_ge(y_out, 16 * NTT)

        @block.vector
        def _(dve):
            tt, stt, ts = nc.vector.tensor_tensor, nc.vector.scalar_tensor_tensor, nc.vector.tensor_scalar
            steps = Steps(dve, dve_step)

            def update(e, scale=1.0, aend=0, used_at=None, deferred=False):
                def low(d):
                    dve.wait_ge(xh_done, 8 * e + d + 1)
                    stt(XL[:, d, :], X[:, d, :], gain(norm_of[e], d), XH[:, d, :].bitcast(F32), ALU.mult, ALU.subtract)\
                        .then_inc(xl_done, 1)

                def rest(d):
                    dve.wait_ge(sq_done, 8 * e + d + 1)
                    if d == 0:
                        nc.vector.tensor_copy(ssum[:, :], sq[:, :]).then_inc(ssum_done, 1)
                    else:
                        dve.wait_ge(ssum_done, 8 * e + d)
                        tt(ssum[:, :], ssum[:, :], sq[:, :], ALU.add).then_inc(ssum_done, 1)
                    if e in norm_of and not deferred:
                        low(d)

                for d in range(ND):
                    if e == 0:
                        dve.wait_ge(xt_done, d + 1)
                        nc.vector.tensor_copy(X[:, d, 0:SEQ], PS[d % RING][:, 0, :])
                        nc.vector.tensor_copy(X[:, d, SEQ:TOK], PS[d % RING][:, 1, 0:NS]).then_inc(x_upd, 1)
                    else:
                        dve.wait_ge(w_used, used_at(d))
                        stt(halves(X[:, d, :]), acc(aend + d % 2), scale, halves(X[:, d, :]), ALU.mult, ALU.add)\
                            .then_inc(x_upd, 1)
                    rest(d)
                if deferred:
                    for d in range(ND):
                        low(d)

            def rms(e):
                dve.wait_ge(stat_done, e + 1)
                ts(halves(rstd[:, :]), STAT[:, :, 0:HALF], 1.0 / D, EPS, ALU.mult, ALU.add).then_inc(var_done, 1)
                dve.wait_ge(sd_done, e + 1)
                nc.vector.reciprocal(rstd[:, :], rstd[:, :]).then_inc(rstd_done, 1)
                dve.wait_ge(rstd_done, e + 1)

            def ffn(name):
                n0, a0, e = at[name]
                rms(e - 1)
                with dve.Fori(0, NF // RING) as i:
                    steps.loop(i, 2 * RING)
                    for j in range(RING):
                        k = 2 * RING * i
                        a, n = a0 + 2 * j, n0 + 2 * j
                        g = gs[:, j % 2, :]
                        dve.wait_ge(w_used, used(n) + k)
                        tt(halves(g), acc(a), halves(rstd[:, :]), ALU.mult).then_inc(acc_evac, 1)
                        dve.wait_ge(w_used, used(n + 1) + k)
                        dve.wait_ge(gh_ready, gh_base(name) + j + RING * i)
                        tt(halves(us[:, :]), acc(a + 1), halves(rstd[:, :]), ALU.mult).then_inc(acc_evac, 1)
                        dve.wait_ge(acc_evac, RING + a + 2 + k)
                        dve.wait_ge(silu_done, gh_base(name) + j + RING * i)
                        steps.done(tt(us[:, :], us[:, :], g, ALU.mult))
                        f = bass.ds(i * RING + j, 1)
                        steps.done(nc.vector.tensor_copy(GH[:, f, :].rearrange("p a t -> p (a t)"), us[:, :]))
                        tt(GL[:, f, :].rearrange("p a t -> p (a t)"), us[:, :],
                           GH[:, f, :].rearrange("p a t -> p (a t)").bitcast(F32), ALU.subtract).then_inc(gh_ready, 1)
                steps.end(NF // RING)
                dve.wait_ge(gh_ready, gh_base(name) + NF)
                update(e, 0.5, a0 + GU_CHUNKS, lambda d: used(n0 + GU_CHUNKS + RING * d + RING - 1))

            def project(n, a, outs):
                dve.wait_ge(w_used, used(n))
                for k, (rows, dst, factor) in enumerate(outs):
                    src, r = acc(a)[rows], halves(rstd[rows, :])
                    if factor == 1.0:
                        ins = tt(halves(dst), src, r, ALU.mult)
                    else:
                        ins = stt(halves(dst), src, factor, r, ALU.mult, ALU.mult)
                ins.then_inc(acc_evac, 1)

            def block_diagonal(m, ms, aend):
                steps.done(nc.vector.memset(m["qbd"][:, :, :], 0.0))
                dve.wait_ge(acc_evac, aend + RING)
                for n in range(KVH):
                    h = slice(n * HD, (n + 1) * HD)
                    dst = m["qbd"][h].rearrange("p b (n g t) -> p n g b t", n=KVH, g=GRP)[:, n]
                    ins = nc.vector.tensor_copy(dst, m["qT"][h, :, SEQ:TOK].rearrange("p g (b t) -> p g b t", b=NB))
                ins.then_inc(ms["qbd_set"], 1)

            def select(scores, mask, done):
                ts(mask, scores, TAKEN / 2, MASK, ALU.is_gt, ALU.mult).then_inc(done, 1)

            def top8(scores, mx8):
                steps.done(nc.vector.max(mx8, scores))
                if steps.i is not None:
                    dve.sem_inc(carried, 1)
                steps.done(nc.vector.match_replace(scores, mx8, scores, TAKEN))

            def prompt_attention(L, m, ms, between, after):
                units = [(i, g) for i in range(NQT) for g in range(GRP)]

                def finish(i):
                    dve.wait_ge(ms["p_set"], 2 * GRP * (i + 1))
                    rs, ri = m["rs"][:, i], m["ri"][:, i]
                    if L == "B":
                        dve.wait_ge(ms["es_set"], i + 1)
                        steps.done(tt(rs, rs, m["es"][:, :, :], ALU.add))
                    steps.done(nc.vector.reciprocal(ri, rs))
                    dve.wait_ge(ms["pv_ps"], 2 * GRP * (i + 1))
                    for n in range(KVH):
                        tt(m["otok"][:, :, n, :], bank[6 + n].rearrange("p (g d) -> p g d", g=GRP),
                           m["ri"][:, i, n, :].unsqueeze(2).to_broadcast([P, GRP, HD]), ALU.mult)\
                            .then_inc(ms["o_evac"], 1)
                    for h in range(2):
                        dve.wait_ge(ms["ot_ps"], 2 * i + h + 1)
                        s = (slice(0, P), slice(4 * h, 4 * h + 4), slice(i * P, (i + 1) * P))
                        src = bank[4 + h].rearrange("p (g t) -> p g t", g=4)
                        steps.done(nc.vector.tensor_copy(XH[s], src))
                        tt(XL[s], src, XH[s].bitcast(F32), ALU.subtract).then_inc(ms["ot_evac"], 1)

                for u, (i, g) in enumerate(units):
                    if g == 0:
                        between(i)
                    k0, nk = key_range(L, i)
                    w = min(nk, 2 * P)
                    dve.wait_ge(ms["qk_ps"], u + 1)
                    near = PS[u % 2][:, :, nk - w:nk]
                    steps.done(tt(near, near, m["strip"][:, :, g, 2 * P - w:2 * P], ALU.add))
                    nm = m["nm"][:, i, :, g]
                    ins = nc.vector.tensor_reduce(nm, PS[u % 2][:, :, 0:nk], AX, ALU.max, negate=True)
                    if L == "B":
                        steps.done(ins)
                        ins = tt(nm, nm, m["nsink"][:, :, g], ALU.min)
                    ins.then_inc(ms["nm_set"], 1)
                    if L == "B" and g == GRP - 1:
                        dve.wait_ge(ms["nm_set"], u + 1)
                        if i:
                            dve.wait_ge(ms["es_set"], i)
                        tt(m["es"][:, :, :], m["nm"][:, i], m["nsink"][:, :, :], ALU.subtract).then_inc(ms["es_in"], 1)
                    if g == 1 and i:
                        finish(i - 1)
                    after(u)
                finish(NQT - 1)

            def paged_sample_attention(m, ms):
                ring, LG = sample_order(), sample_logits

                def maxima(b):
                    dve.wait_ge(ms["qkS_ps"], b + 1)
                    steps.done(tt(LG[:, KEYS - NEAR:KEYS], LG[:, KEYS - NEAR:KEYS], m["biasS"][:, :], ALU.add))
                    nc.vector.tensor_reduce(m["nmS"][:, b:b + 1], LG[:, 0:KEYS], AX, ALU.max, negate=True)\
                        .then_inc(ms["nmS_set"], 1)

                def outputs(b):
                    dve.wait_ge(ms["otS_ps"], b + 1)
                    part = []
                    for n in range(KVH):
                        h = slice(n * HD, (n + 1) * HD)
                        part.append((bank[7][h, P + n * HD:P + (n + 1) * HD].rearrange("p (g t) -> p g t", g=GRP),
                                     (h, slice(0, GRP), slice(SEQ + b * NT, SEQ + (b + 1) * NT))))
                    for src, s in part:
                        steps.mark(nc.vector.tensor_copy(XH[s], src))
                    steps.settle()
                    for src, s in part:
                        ins = tt(XL[s], src, XH[s].bitcast(F32), ALU.subtract)
                    ins.then_inc(ms["otS_evac"], 1)

                maxima(0)
                for b in range(NB):
                    if b + 1 < NB:
                        maxima(b + 1)
                    if b:
                        outputs(b - 1)
                        dve.wait_ge(ms["pvS_ps"], b)
                    for k, tiles in enumerate(PT_TILES):
                        dve.wait_ge(ms["ptS_ps"], b * PT_GROUPS + k + 1)
                        bk = bank[5 + ring.index(("pt", b, k)) % 2]
                        full = [j for j in tiles if j < NPG]
                        if full:
                            ins = nc.vector.tensor_copy(m["pts"][:, full[0]:full[-1] + 1, :],
                                                        bk[:, 0:len(full) * P].rearrange("p (a b) -> p a b", b=P))
                        if len(full) < len(tiles):
                            c = len(full) * P
                            ins = nc.vector.tensor_copy(m["pts"][0:NT, NPG, :], bk[0:NT, c:c + P])
                        ins.then_inc(ms["ptS_evac"], 1)
                    ri = m["riS"][:, b:b + 1]
                    steps.done(nc.vector.reciprocal(ri, m["rsS"][:, b:b + 1]))
                    dve.wait_ge(ms["pvS_ps"], b + 1)
                    ts(m["os"][:, :], bank[7][:, 0:P], ri, None, ALU.mult).then_inc(ms["osS_set"], 1)
                outputs(NB - 1)

            def window_sample_attention(m, ms):
                for k, group in enumerate(LOGIT_GROUPS):
                    dve.wait_ge(ms["qkS_ps"], k + 1)
                    n = len(group)
                    lg = bank[k][:, 0:n * NEAR].rearrange("p (b x) -> p b x", b=n)
                    steps.done(tt(lg, lg, m["biasS"][:, :].unsqueeze(1).to_broadcast([P, n, NEAR]), ALU.add))
                    nm = m["nmS"][:, group[0]:group[0] + n]
                    steps.done(nc.vector.tensor_reduce(nm, lg, AX, ALU.max, negate=True))
                    tt(nm, nm, m["nsinkS"][:, :].to_broadcast([P, n]), ALU.min).then_inc(ms["nmS_set"], 1)
                dve.wait_ge(ms["nmS_set"], len(LOGIT_GROUPS))
                tt(m["esS"][:, :], m["nmS"][:, :], m["nsinkS"][:, :].to_broadcast([P, NB]), ALU.subtract)\
                    .then_inc(ms["esS_in"], 1)
                for half in range(2):
                    dve.wait_ge(ms["ptS_ps"], half + 1)
                    nc.vector.tensor_copy(m["pts"][:, half * HALF_B:(half + 1) * HALF_B, :].rearrange(
                        "p b k -> p (b k)"), bank[5 + half][:, :]).then_inc(ms["ptS_evac"], 1)
                dve.wait_ge(ms["esS_set"], 1)
                steps.done(tt(m["rsS"][:, :], m["rsS"][:, :], m["esS"][:, :], ALU.add))
                steps.done(nc.vector.reciprocal(m["riS"][:, :], m["rsS"][:, :]))
                for half in range(2):
                    dve.wait_ge(ms["pvS_ps"], half + 1)
                    of = slice(half * HALF_B, (half + 1) * HALF_B)
                    tt(m["os"][:, of, :], bank[(4, 0)[half]].rearrange("p (b d) -> p b d", b=HALF_B),
                       m["riS"][:, of].unsqueeze(2).to_broadcast([P, HALF_B, P]), ALU.mult).then_inc(ms["osS_set"], 1)
                for half in range(2):
                    dve.wait_ge(ms["otS_ps"], half + 1)
                    part = []
                    for n in range(KVH):
                        h = slice(n * HD, (n + 1) * HD)
                        src = bank[1 + half][h, :].rearrange("p (b c) -> p b c", b=HALF_B)[:, :, n * HD:(n + 1) * HD]
                        t0 = SEQ + half * HALF_B * NT
                        high, low = (Z[h, 0:GRP, t0:t0 + HALF_B * NT].rearrange("p g (b t) -> p g b t", b=HALF_B)
                                     for Z in (XH, XL))
                        part.append((src.rearrange("p b (g t) -> p g b t", g=GRP), high, low))
                    for src, high, low in part:
                        steps.mark(nc.vector.tensor_copy(high, src))
                    steps.settle()
                    for src, high, low in part:
                        ins = tt(low, src, high.bitcast(F32), ALU.subtract)
                    ins.then_inc(ms["otS_evac"], 1)

            nc.vector.memset(tabx[NBUCK:NBUCK + 1, :], MASK)
            nc.vector.memset(ones[:, :], 1.0).then_inc(ones_set, 1)
            dve.wait_ge(gain_set, 1)
            update(0)
            ffn("ffn0")
            m, ms = mixers["A"], MS["A"]
            n0, a0, e = at["inA"]
            rms(e - 1)
            lo, hi, both = slice(0, IDIM), slice(IDIM, 2 * IDIM), slice(0, P)
            wi = slice(IDIM, IDIM + IH)
            project(n0, a0, [(lo, m["kiT"][lo, :], 1.0), (lo, m["kiT"][hi, :], 1.0), (wi, sq[wi, :], 1.0)])
            for c in range(IH // 2):
                project(n0 + 1 + c, a0 + 1 + c, [(both, m["qiT"][:, c, :], 1.0)])
            dve.wait_ge(acc_evac, a0 + 1 + IH // 2 + RING)
            for src in range(2):
                for dst in range(2):
                    s, d = slice(src * 64, src * 64 + 64), slice(dst * 64, dst * 64 + 64)
                    for c in range(IH // 2):
                        ins = nc.vector.tensor_copy(m["qiS"][d, :, 2 * c + src, :],
                                                    m["qiT"][s, c, SEQ:TOK].rearrange("p (b t) -> p b t", b=NB))
            ins.then_inc(ms["qis_set"], 1)
            dve.wait_ge(ms["rep_ps"], 1)
            dve.wait_ge(ms["mix_in"], 16 * N_MIX["A"])
            for j in range(NB // 2):
                ins = tt(m["wbl"][:, j, :], bank[7][:, 0:NS], m["pairm"][:, j, :], ALU.mult)
            ins.then_inc(ms["wbl_set"], 1)
            dve.wait_ge(ms["kiw_sb"], 1)
            steps.done(ts(m["wis"][:, :, :], m["kiw"][:, 0:NQT, IDIM:IDIM + IH], IH ** -0.5, None, ALU.mult))
            scs = m["scs"]
            pages = scs[:, 0:PAST].rearrange("s (r e c) -> s r e c", e=2, c=PAGE)
            for k in range(5):
                dve.wait_ge(ms["r_usedS"], (k + 1) * NB // 2)
                bk = bank[4 + k % 2]
                if k < 4:
                    nc.vector.tensor_copy(pages[:, 4 * (k // 2):4 * (k // 2) + 4, k % 2, :],
                                          bk[0:NS, :].rearrange("s (r c) -> s r c", r=4)).then_inc(ms["s_evac"], 1)
                else:
                    tt(scs[:, PAST:KEYS], bk[0:NS, 0:NT], m["tailm"][:, :], ALU.add).then_inc(ms["s_evac"], 1)
            k = rounds = 0
            dve.wait_ge(ms["s_evac"], 5)
            for i in range(1, NQT):
                s = m["scp"][:, i - 1, 0:(i + 1) * P]
                for h in range(IH):
                    dve.wait_ge(ms["r_set"], 5 * NB // 2 + k + 1)
                    r, w = m["r"][:, k % 2, 0:(i + 1) * P], m["wis"][:, i, h:h + 1]
                    if h == 0:
                        ins = ts(s, r, w, None, ALU.mult)
                    else:
                        dve.wait_ge(ms["r_usedP"], k)
                        ins = stt(s, r, w, s, ALU.mult, ALU.add)
                    ins.then_inc(ms["r_usedP"], 1)
                    k += 1
                dve.wait_ge(ms["r_usedP"], k)
                diag = m["scp"][:, i - 1, i * P:(i + 1) * P]
                ins = tt(diag, diag, m["cmask"][:, :], ALU.add)
                ins.then_inc(ms["cm_used"], 1)
                top8(scs[:, :], m["mx8"][0:NS, :])
                rounds += 1
            dve.wait_ge(ms["cm_used"], NQT - 1)
            c = 1 + IH // 2
            for k, name in enumerate(("kT", "vT")):
                top8(scs[:, :], m["mx8"][0:NS, :])
                project(n0 + c + k, a0 + c + k, [(both, m[name][:, :], 1.0)])
                rounds += 1
            for g in range(GRP):
                project(n0 + c + 2 + g, a0 + c + 2 + g, [(both, m["qT"][:, g, :], HD ** -0.5)])
                top8(scs[:, :], m["mx8"][0:NS, :])
                rounds += 1
            block_diagonal(m, ms, a0 + A_CHUNKS)

            def strips(i):
                if i == 0:
                    dve.wait_ge(ms["strip_in"], 16 * (1 + HEADS))

            def selections(u):
                i, g = divmod(u, GRP)
                s = m["scp"][:, i, 0:(i + 2) * P] if i + 1 < NQT else None
                of_prompt = 0 if s is None else 2 * ROUNDS_AFTER[g]
                of_sample = 2 if u in sample_units else 0

                def step(k, scores, mx8):
                    if k % 2 == 0:
                        steps.mark(nc.vector.max(mx8, scores))
                    else:
                        steps.mark(nc.vector.match_replace(scores, mx8, scores, TAKEN))

                for k in range(max(of_prompt, of_sample)):
                    if k < of_prompt:
                        if k:
                            dve.wait_ge(dve_step, prompt_done)
                        step(k, s, m["mx8p"][:, :])
                        prompt_done = steps.n
                    if k < of_sample:
                        if k:
                            dve.wait_ge(dve_step, sample_done)
                        step(k, scs[:, :], m["mx8"][0:NS, :])
                        sample_done = steps.n
                steps.settle()
                if s is not None and g == LAST_ROUNDS:
                    select(s, m["pmask"][:, i, 0:(i + 2) * P], ms["pmask_set"])
                if u == sample_units[-1]:
                    select(scs[:, :], m["maskS"][:, :], ms["maskS_set"])

            early = (NQT - 1) * GRP
            left = TOPK_S // 8 - rounds
            late = min(left, GRP - 1)
            sample_units = [k * early // (left - late) for k in range(left - late)] + \
                [early + k for k in range(late)]
            assert left - late <= early
            prompt_attention("A", m, ms, strips, selections)
            paged_sample_attention(m, ms)
            n1, _, e = at["outA"]
            update(e, 1.0, a0 + A_CHUNKS, lambda d: used(n1 + d), deferred=True)
            ffn("ffn1")
            ffn("ffn2")
            m, ms = mixers["B"], MS["B"]
            n0, a0, e = at["inB"]
            rms(e - 1)
            project(n0, a0, [(both, m["kT"][:, :], 1.0)])
            project(n0 + 1, a0 + 1, [(both, m["vT"][:, :], 1.0)])
            for g in range(GRP):
                project(n0 + 2 + g, a0 + 2 + g, [(both, m["qT"][:, g, :], HD ** -0.5)])
            block_diagonal(m, ms, a0 + B_CHUNKS)
            dve.wait_ge(ms["mix_in"], 16 * N_MIX["B"])
            dve.wait_ge(ms["strip_in"], 16 * (1 + HEADS))
            steps.mark(tt(m["nsink"][:, :, :], m["es"][:, :, :], m["nsink"][:, :, :], ALU.subtract))
            steps.mark(tt(m["nsinkS"][:, :], m["esS"][:, 0:1], m["nsinkS"][:, :], ALU.subtract))
            steps.mark(tt(m["biasS"][:, :], m["biasS"][:, :], m["wmS"][:, :], ALU.add))
            for n in range(KVH):
                far = m["strip"][:, n, :, 0:P]
                steps.mark(tt(far, far, m["wm"][:, :].unsqueeze(1).to_broadcast([P, GRP, P]), ALU.add))
            steps.settle()
            prompt_attention("B", m, ms, lambda i: None, lambda u: None)
            window_sample_attention(m, ms)
            n1, _, e = at["outB"]
            update(e, 1.0, a0 + B_CHUNKS, lambda d: used(n1 + d), deferred=True)
            ffn("ffn3")
            rms(6)
            for d in range(ND):
                stt(X[:, d, :], X[:, d, :], gain(6, d), rstd[:, :], ALU.mult, ALU.mult).then_inc(fin_x, 1)


LAST_ROUNDS = GRP - 3
ROUNDS_AFTER = [TOPK_P // 8 * (g + 1) // (LAST_ROUNDS + 1) - TOPK_P // 8 * g // (LAST_ROUNDS + 1)
                if g <= LAST_ROUNDS else 0 for g in range(GRP)]
KV_SLOTS = 3
HALF_B = NB // 2
LOGIT_GROUPS = [list(range(NB))[k:k + 3] for k in range(0, NB, 3)]


def key_range(L, i):
    first = 0 if L == "A" else max(0, i - 1) * P
    return first, (i + 1) * P - first


KT_TILES = [list(range(NPG))[k:k + 4] for k in range(0, NPG, 4)]
PT_TILES = [list(range(NPG + 1))[k:k + 4] for k in range(0, NPG + 1, 4)]
KT_GROUPS, PT_GROUPS = len(KT_TILES), len(PT_TILES)


def sample_order():
    ring = [("kt", b, k) for b in range(2) for k in range(KT_GROUPS)]
    for b in range(NB):
        ring += [("pt", b, k) for k in range(PT_GROUPS)]
        if b + 2 < NB:
            ring += [("kt", b + 2, k) for k in range(KT_GROUPS)]
    return ring


def constants():
    p, c = np.arange(P)[:, None], np.arange(P)[None, :]
    coef = np.zeros((NBUCK + 1, GW), np.float32)
    half = NBUCK // 2
    for m in range(GW):
        n = 2 * P - 1 - m
        if n < 0:
            coef[NBUCK, m] = 1.0
            continue
        log = np.log(np.float32(max(n, 1)) / np.float32(half)) / np.float32(math.log(MAXD / half))
        bucket = n if n < half else min(half + int(log * np.float32(NBUCK - half)), NBUCK - 1)
        coef[bucket, m] += 1.0
        coef[NBUCK - 1, m] -= 1.0
    rep = np.zeros((P, P), np.float32)
    pairm = np.zeros((P, NB // 2, NS), np.float32)
    selb = np.zeros((NS, NB, P), np.float32)
    for bb in range(2):
        for h in range(IH):
            for t in range(NT):
                row = bb * 64 + h * NT + t
                rep[IDIM + h, row] = 1.0
                for j in range(NB // 2):
                    pairm[row, j, (2 * j + bb) * NT + t] = np.float32(IH ** -0.5)
    for b in range(NB):
        for row in range(P):
            selb[b * NT + row % NT, b, row] = 1.0
    ns = np.arange(NS)[:, None]
    return {
        "c_ident": np.eye(P, dtype=np.float32), "c_coef": coef, "c_rep": rep,
        "c_pairm": pairm.reshape(P, -1), "c_selb": selb.reshape(NS, -1),
        "c_cmask": np.where(c > p, MASK, 0.0).astype(np.float32),
        "c_wmask": np.where(c < p, MASK, 0.0).astype(np.float32),
        "c_tailm": np.where(np.arange(NT)[None, :] > ns % NT, MASK, 0.0).astype(np.float32),
        "c_wmaskS": np.where(np.arange(NEAR)[None, :] < p % NT, MASK, 0.0).astype(np.float32),
    }


N_CONST = 6
N_MIX = {"A": 4, "B": 6}
_OUTS = [("y_prompt", (1, SEQ, D)), ("y_sample", (NB, NT, D)), ("new_kv_prompt", (1, 1, SEQ, 2, KVH, HD)),
         ("new_idx_prompt", (1, 1, SEQ, IDIM)), ("new_win_prompt", (1, 1, P, 2, KVH, HD)),
         ("new_kv_sample", (1, NB, NT, 2, KVH, HD)), ("new_idx_sample", (1, NB, NT, IDIM)),
         ("new_win_sample", (1, NB, P, 2, KVH, HD))]


def kernel(**inputs):
    import concourse.bacc as _bacc
    from concourse.bass_utils import run_bass_kernel_spmd as _run

    nc = _bacc.Bacc("TRN2", target_bir_lowering=False, num_devices=1)
    arrays, io = {}, {}
    given = {name: np.ascontiguousarray(a) for name, a in inputs.items()}
    given.update(constants())
    for name, a in given.items():
        arrays[f"in_{name}"] = a
        io[name] = nc.dram_tensor(f"in_{name}", a.shape, mybir.dt.from_np(a.dtype), kind="ExternalInput").ap()
    for name, shape in _OUTS:
        io[name] = nc.dram_tensor(f"out_{name}", shape, F32, kind="ExternalOutput").ap()
    bass_hybrid_step(nc, io)
    r = _run(nc, [arrays], core_ids=[0])
    return tuple(r.results[0][f"out_{name}"] for name, _ in _OUTS)
```
